# Optimizing a Trainium2 kernel written in Bass

```python
import jax, jax.numpy as jnp
from jax import lax
import numpy as np

D_MODEL = 1024
BATCH = 1
SEQ = 1024
DEPTH = 1

MEM_LEN = 256
EPS = 1e-6
CONV_WIDTH = 3
A_WIDTH = D_MODEL // 2
HEAD_DIM = 64
ATTN_WIDTH = D_MODEL // 2
N_Q_HEADS = ATTN_WIDTH // HEAD_DIM
N_KV_HEADS = N_Q_HEADS // 4
KV_WIDTH = N_KV_HEADS * HEAD_DIM
WINDOW = 128
BLOCK = 128
ROPE_THETA = 500000.0
ROT_DIM = HEAD_DIM // 4
MEM_HEADS = 4
MEM_HEAD_DIM = D_MODEL // 8
MEM_WIDTH = MEM_HEADS * MEM_HEAD_DIM
N_BRANCHES = 3
IN_SIZES = (A_WIDTH, A_WIDTH, A_WIDTH, A_WIDTH,
            ATTN_WIDTH, KV_WIDTH, KV_WIDTH, ATTN_WIDTH,
            MEM_WIDTH, MEM_WIDTH,
            N_BRANCHES * D_MODEL)
IN_WIDTH = sum(IN_SIZES)

kernel_name = "hybrid_gated_conv_swa_memxattn_block"

def rms_norm(x, g):
    xf = x.astype(jnp.float32)
    y = xf * lax.rsqrt(jnp.mean(xf * xf, axis=-1, keepdims=True) + EPS)
    return (y * g.astype(jnp.float32)).astype(x.dtype)

def partial_rope(t, pos):
    half = ROT_DIM // 2
    inv_freq = jnp.power(jnp.float32(ROPE_THETA), -jnp.arange(half, dtype=jnp.float32) * (2.0 / ROT_DIM))
    ang = pos.astype(jnp.float32)[:, None] * inv_freq[None, :]
    cos = jnp.cos(ang)[None, :, None, :]
    sin = jnp.sin(ang)[None, :, None, :]
    tr = t[..., :ROT_DIM].astype(jnp.float32)
    t1, t2 = tr[..., :half], tr[..., half:]
    rot = jnp.concatenate([t1 * cos - t2 * sin, t2 * cos + t1 * sin], axis=-1).astype(t.dtype)
    return jnp.concatenate([rot, t[..., ROT_DIM:]], axis=-1)

def short_gated_conv(b, c, u, w_conv):
    s = u.shape[1]
    cu = jnp.pad(c * u, ((0, 0), (1, 1), (0, 0)))
    y = cu[:, :s] * w_conv[0] + cu[:, 1:s + 1] * w_conv[1] + cu[:, 2:] * w_conv[2]
    return b * y

def window_attention_with_sink(q, k, v, sink):
    bsz, s, hq, dh = q.shape
    hkv = k.shape[2]
    grp = hq // hkv
    nb = s // BLOCK
    qb = q.reshape(bsz, nb, BLOCK, hkv, grp, dh)
    pad = ((0, 0), (BLOCK, BLOCK), (0, 0), (0, 0))
    kp = jnp.pad(k, pad).reshape(bsz, nb + 2, BLOCK, hkv, dh)
    vp = jnp.pad(v, pad).reshape(bsz, nb + 2, BLOCK, hkv, dh)
    kw = jnp.concatenate([kp[:, :nb], kp[:, 1:nb + 1], kp[:, 2:]], axis=2)
    vw = jnp.concatenate([vp[:, :nb], vp[:, 1:nb + 1], vp[:, 2:]], axis=2)
    qpos = jnp.arange(nb)[:, None] * BLOCK + jnp.arange(BLOCK)[None, :]
    kpos = (jnp.arange(nb)[:, None] - 1) * BLOCK + jnp.arange(3 * BLOCK)[None, :]
    valid = ((jnp.abs(qpos[:, :, None] - kpos[:, None, :]) <= WINDOW)
             & (kpos >= 0)[:, None, :] & (kpos < s)[:, None, :])
    scores = jnp.einsum('bnqhgd,bnkhd->bnhgqk', qb, kw,
                        preferred_element_type=jnp.float32) * (dh ** -0.5)
    scores = jnp.where(valid[None, :, None, None], scores, -jnp.inf)
    sink_l = sink.astype(jnp.float32).reshape(hkv, grp)[None, None, :, :, None, None]
    m = jnp.maximum(jnp.max(scores, axis=-1, keepdims=True), sink_l)
    p = jnp.exp(scores - m)
    p = p / (jnp.sum(p, axis=-1, keepdims=True) + jnp.exp(sink_l - m))
    out = jnp.einsum('bnhgqk,bnkhd->bnqhgd', p.astype(v.dtype), vw)
    return out.reshape(bsz, s, hq * dh)

def memory_cross_attention(q, mk, mv):
    dm = q.shape[-1]
    scores = jnp.einsum('bshd,bmhd->bhsm', q, mk,
                        preferred_element_type=jnp.float32) * (dm ** -0.5)
    p = jax.nn.softmax(scores, axis=-1)
    out = jnp.einsum('bhsm,bmhd->bshd', p.astype(mv.dtype), mv)
    return out.reshape(q.shape[0], q.shape[1], -1)

def hybrid_layer(x, mem, g_pre, w_in, w_conv, attn_sink, g_mem, w_mem_kv,
                 w_up_a, w_up_b, w_up_m, w_out, g_post):
    bsz, s, d = x.shape
    h = rms_norm(x, g_pre)
    proj = h @ w_in
    idx = list(np.cumsum(IN_SIZES)[:-1])
    (a_b, a_c, a_x, a_z, b_q, b_k, b_v, b_z, m_q, m_z, gate_logits) = jnp.split(proj, idx, axis=-1)

    ya = short_gated_conv(a_b, a_c, a_x, w_conv) * jax.nn.silu(a_z)
    ua = ya @ w_up_a

    pos = jnp.arange(s)
    q = partial_rope(b_q.reshape(bsz, s, N_Q_HEADS, HEAD_DIM), pos)
    k = partial_rope(b_k.reshape(bsz, s, N_KV_HEADS, HEAD_DIM), pos)
    v = b_v.reshape(bsz, s, N_KV_HEADS, HEAD_DIM)
    yb = window_attention_with_sink(q, k, v, attn_sink) * jax.nn.silu(b_z)
    ub = yb @ w_up_b

    mn = rms_norm(mem, g_mem)
    mkv = mn @ w_mem_kv
    mk, mv = jnp.split(mkv, 2, axis=-1)
    mlen = mem.shape[1]
    ym = memory_cross_attention(m_q.reshape(bsz, s, MEM_HEADS, MEM_HEAD_DIM),
                                mk.reshape(bsz, mlen, MEM_HEADS, MEM_HEAD_DIM),
                                mv.reshape(bsz, mlen, MEM_HEADS, MEM_HEAD_DIM)) * jax.nn.silu(m_z)
    um = ym @ w_up_m

    gates = jax.nn.sigmoid(gate_logits.astype(jnp.float32)).astype(x.dtype).reshape(bsz, s, N_BRANCHES, d)
    merged = gates[:, :, 0] * ua + gates[:, :, 1] * ub + gates[:, :, 2] * um
    out = merged @ w_out
    return x + rms_norm(out, g_post)

def setup_inputs(seed: int = 0) -> dict:
    key = jax.random.key(seed)
    ks = jax.random.split(key, 14)
    f32 = jnp.float32
    nrm = lambda k, shape, fan_in: jax.random.normal(k, shape, f32) * (fan_in ** -0.5)
    gain = lambda k, shape: 1.0 + 0.05 * jax.random.normal(k, shape, f32)
    return {
        "x": jax.random.normal(ks[0], (BATCH, SEQ, D_MODEL), f32),
        "mem": jax.random.normal(ks[1], (BATCH, MEM_LEN, D_MODEL), f32),
        "g_pre": gain(ks[2], (DEPTH, D_MODEL)),
        "w_in": nrm(ks[3], (DEPTH, D_MODEL, IN_WIDTH), D_MODEL),
        "w_conv": nrm(ks[4], (DEPTH, CONV_WIDTH, A_WIDTH), CONV_WIDTH),
        "attn_sink": 0.5 * jax.random.normal(ks[5], (DEPTH, N_Q_HEADS), f32),
        "g_mem": gain(ks[6], (DEPTH, D_MODEL)),
        "w_mem_kv": nrm(ks[7], (DEPTH, D_MODEL, 2 * MEM_WIDTH), D_MODEL),
        "w_up_a": nrm(ks[8], (DEPTH, A_WIDTH, D_MODEL), A_WIDTH),
        "w_up_b": nrm(ks[9], (DEPTH, ATTN_WIDTH, D_MODEL), ATTN_WIDTH),
        "w_up_m": nrm(ks[10], (DEPTH, MEM_WIDTH, D_MODEL), MEM_WIDTH),
        "w_out": nrm(ks[11], (DEPTH, D_MODEL, D_MODEL), D_MODEL),
        "g_post": gain(ks[12], (DEPTH, D_MODEL)),
    }

def reference(x, mem, g_pre, w_in, w_conv, attn_sink, g_mem, w_mem_kv,
              w_up_a, w_up_b, w_up_m, w_out, g_post):
    for l in range(DEPTH):
        x = hybrid_layer(x, mem, g_pre[l], w_in[l], w_conv[l], attn_sink[l], g_mem[l],
                         w_mem_kv[l], w_up_a[l], w_up_b[l], w_up_m[l], w_out[l], g_post[l])
    return x


_drawn_inputs = setup_inputs


def setup_inputs(seed=0):
    import zlib

    import numpy as np

    out = dict(_drawn_inputs(seed))
    spreads = {}
    factors = {'attn_sink': 64.0, 'g_mem': 8.0, 'w_up_b': 5.012}
    for name, (base, spread) in spreads.items():
        noise = np.random.default_rng([zlib.crc32(name.encode()), seed]).standard_normal(out[name].shape)
        drawn = base * np.exp(spread * noise) if base else spread * noise
        out[name] = __import__('jax').numpy.asarray(drawn.astype(out[name].dtype))
    for name, factor in factors.items():
        out[name] = (out[name] * factor).astype(out[name].dtype)
    return out
```

```python
from contextlib import ExitStack, contextmanager

import numpy as np

import concourse.bass as bass
from concourse import mybir

P = 128
D = 1024
SEQ = 1024
KC = D // P
NB = SEQ // P
HALF = 512
AW = D // 2
AC = AW // P
HEAD = 64
GROUP = 4
HEADS = 8
MEM = 256
MHEADS = 4
WIN = 3 * P
EPS = 1e-6
ROPE_THETA = 500000.0
ROT = HEAD // 4

F32 = mybir.dt.float32
F32R = mybir.dt.float32r
ALU = mybir.AluOpType
ACT = mybir.ActivationFunctionType
AX = mybir.AxisListType

T_QKV = 0
T_CONV = T_QKV + 2 + AC
T_MA = T_CONV + 4 * AC
T_ZB = T_MA + 2 * KC
T_MQ = T_ZB + AC
T_MEM = T_MQ + AC
T_MB = T_MEM + 2 * MHEADS
T_ZM = T_MB + 2 * KC
T_MM = T_ZM + AC
T_OUT = T_MM + 2 * KC

Q0, K0, V0, QZ0, P0, PT0, VW0, SIG0, AREA_A = 0, 4096, 5120, 6144, 7168, 8704, 10240, 11008, 12032
CS0, CU0, TA0 = 6144, 7168, 8200
MK0, MV0, MX0, MN0 = 4096, 5120, 6144, 8192
MP0, MPT0, MQZ0 = 6144, 7168, 10240
GP0, TO0 = 8192, 9216
QRAW0, SWAP0, COS0, SIN0, ROT0, VT0 = 0, 1024, 2048, 3072, 4096, 5120


def split_index(t):
    return t if t < T_MEM else t - 2 * MHEADS


def await_count(eng, sem, count):
    if not (isinstance(count, int) and count == 0):
        eng.wait_ge(sem, count)


class Chain:

    def __init__(self, eng, sem):
        self.eng, self.sem, self.base, self.inside, self.turn = eng, sem, 0, 0, None

    def link(self, ins):
        self.inside += 1
        ins.then_inc(self.sem, 1)
        at = self.base + self.inside
        if self.turn is not None:
            i, first, per = self.turn
            at = (i - first) * per + at if first else i * per + at
        self.eng.wait_ge(self.sem, at)

    @contextmanager
    def loop(self, first, end, per):
        self.base, self.inside = self.base + self.inside, 0
        with self.eng.Fori(first, end) as i:
            self.turn = (i, first, per)
            yield i
        assert self.inside == per, (self.inside, per)
        self.base, self.inside, self.turn = self.base + per * (end - first), 0, None


def hybrid_layer(nc, x, mem, w8, wup, wmem, wout, g_pre, g_mem, g_post, w_conv, sink,
                 cos, sin, mask, ident_in, out):
    ctx = ExitStack()
    with ctx:
        def sb(name, shape, dt=F32):
            return ctx.enter_context(nc.sbuf_tensor(name, shape, dt))

        def psum(name, shape):
            return ctx.enter_context(nc.psum_tensor(name, shape, F32))

        def sem(name):
            return ctx.enter_context(nc.semaphore(name))

        h_hi = sb("h_hi", [P, KC, SEQ], F32R)
        h_lo = sb("h_lo", [P, KC, SEQ], F32R)
        y_hi = sb("y_hi", [P, AC, SEQ], F32R)
        y_lo = sb("y_lo", [P, AC, SEQ], F32R)
        area_m = sb("area_m", [P, KC * SEQ])
        raw = sb("raw", [P, 2, D])
        w_hi = sb("w_hi", [P, 2, D], F32R)
        w_lo = sb("w_lo", [P, 2, D], F32R)
        area_a = sb("area_a", [P, AREA_A])
        maskb = sb("maskb", [P, 5 * P])
        ident = sb("ident", [P, P])
        gpre = sb("gpre", [P, KC])
        gmem = sb("gmem", [P, KC])
        wconv = sb("wconv", [P, 3, AC])
        sinkb = sb("sinkb", [P, HEADS])
        st = sb("st", [P, 12, 8])

        merged = area_m[:, :].rearrange("p (k s) -> p k s", k=KC)
        qT = area_a[:, Q0:K0].rearrange("p (c s) -> p c s", c=AC)
        kT = area_a[:, K0:K0 + SEQ]
        vtok = area_a[:, V0:V0 + SEQ].rearrange("p (b d) -> p b d", b=NB)
        qz = area_a[:, QZ0:QZ0 + 2 * GROUP * P].rearrange("p (g h q) -> p g h q", g=2, h=GROUP)
        probs = area_a[:, P0:P0 + GROUP * WIN].rearrange("p (h k) -> p h k", h=GROUP)
        probsT = area_a[:, PT0:PT0 + 3 * GROUP * P].rearrange("p (j h q) -> p j h q", j=3, h=GROUP)
        vwin = area_a[:, VW0:VW0 + 3 * 2 * P].rearrange("p (j g d) -> p j g d", j=3, g=2)
        sig = area_a[:, SIG0:SIG0 + SEQ]
        conv_c = area_a[:, CS0:CS0 + SEQ]
        conv_cu = area_a[:, CU0:CU0 + SEQ + 2]
        conv_t = area_a[:, TA0:TA0 + SEQ]
        q_raw = area_m[:, QRAW0:QRAW0 + SEQ]
        q_swap = area_m[:, SWAP0:SWAP0 + SEQ]
        cosb = area_m[:, COS0:COS0 + SEQ]
        sinb = area_m[:, SIN0:SIN0 + SEQ]
        rot_t = area_m[:, ROT0:ROT0 + SEQ]
        vT = area_m[:, VT0:VT0 + SEQ]
        mkT = area_a[:, MK0:MK0 + MHEADS * MEM].rearrange("p (h m) -> p h m", h=MHEADS)
        mv = area_a[:, MV0:MV0 + 2 * AW].rearrange("p (b d) -> p b d", b=2)
        memx = area_a[:, MX0:MX0 + 2 * D].rearrange("p (b d) -> p b d", b=2)
        mnT = area_a[:, MN0:MN0 + KC * MEM].rearrange("p (k m) -> p k m", k=KC)
        mprobs = area_a[:, MP0:MP0 + MHEADS * MEM].rearrange("p (h m) -> p h m", h=MHEADS)
        mprobsT = area_a[:, MPT0:MPT0 + 2 * MHEADS * P].rearrange("p (b h q) -> p b h q", b=2, h=MHEADS)
        mqz = area_a[:, MQZ0:MQZ0 + MHEADS * P].rearrange("p (h q) -> p h q", h=MHEADS)
        wout_raw = area_a[:, 0:KC * D]
        gpostb = area_a[:, GP0:GP0 + D]
        tout = area_a[:, TO0:TO0 + 2 * D].rearrange("p (b d) -> p b d", b=2)
        wo_hi = h_hi[:, :, :].rearrange("p k s -> p (k s)")
        wo_lo = h_lo[:, :, :].rearrange("p k s -> p (k s)")
        mb_hi = y_hi[:, :, :].rearrange("p c s -> p (c s)")
        mb_lo = y_lo[:, :, :].rearrange("p c s -> p (c s)")

        pm = psum("pm", [P, 2, SEQ])
        sa = psum("sa", [P, 3, HALF])
        pv = psum("pv", [P, HALF])

        x_landed = [sem(f"x_landed{b}") for b in range(NB)]
        small_landed = sem("small_landed")
        rope_landed = sem("rope_landed")
        mem_landed = sem("mem_landed")
        gpost_landed = sem("gpost_landed")
        wout_landed = [sem(f"wout_landed{n}") for n in range(2)]
        raw_landed = [sem(f"raw_landed{p}") for p in range(2)]
        xres_landed = [sem(f"xres_landed{p}") for p in range(2)]
        stored = [sem(f"stored{p}") for p in range(2)]
        ssq_act = sem("ssq_act")
        var_made, root_made, xs_made = sem("var_made"), sem("root_made"), sem("xs_made")
        x_turned, h_hi_made, h_made = sem("x_turned"), sem("h_hi_made"), sem("h_made")
        hi_made, lo_made = sem("hi_made"), sem("lo_made")
        tile_done = sem("tile_done")
        drained = [sem(f"drained{p}") for p in range(2)]
        swapped, roped = sem("swapped"), sem("roped")
        v_turned, v_made = sem("v_turned"), sem("v_made")
        sig_made, y_made, y_hi_made, y_ready = sem("sig_made"), sem("y_made"), sem("y_hi_made"), sem("y_ready")
        q_staged, v_staged = sem("q_staged"), sem("v_staged")
        scored, masked, nm_ready, exped = sem("scored"), sem("masked"), sem("nm_ready"), sem("exped")
        p_ready, turned, pt_act, pt_dve = sem("p_ready"), sem("turned"), sem("pt_act"), sem("pt_dve")
        pv_done, o_taken = sem("pv_done"), sem("o_taken")
        memx_ready, mem_turned, mn_made = sem("memx_ready"), sem("mem_turned"), sem("mn_made")
        mq_staged, mscored, mnm_ready, mexped = sem("mq_staged"), sem("mscored"), sem("mnm_ready"), sem("mexped")
        mp_ready, mturned, merged_done = sem("mp_ready"), sem("mturned"), sem("merged_done")
        wo_hi_made, wo_lo_made = sem("wo_hi_made"), sem("wo_lo_made")
        mb_hi_made, mb_lo_made = sem("mb_hi_made"), sem("mb_lo_made")
        sq_made, out_var, out_root, out_ready = sem("sq_made"), sem("out_var"), sem("out_root"), sem("out_ready")
        act_chain, dve_chain = sem("act_chain"), sem("dve_chain")

        block = ctx.enter_context(nc.Block())

        @block.sync
        def _(sp):
            for b in range(NB):
                sp.dma_start(area_m[:, b * D:(b + 1) * D], x[b * P:(b + 1) * P, :]).then_inc(x_landed[b], 16)
                if b == 1:
                    for dst, src in ((ident[:, :], ident_in), (gpre[:, :], g_pre), (gmem[:, :], g_mem),
                                     (wconv[:, :, :], w_conv), (sinkb[:, :], sink), (maskb[:, :], mask)):
                        sp.dma_start(dst, src).then_inc(small_landed, 16)
                if b == 3:
                    for p in range(2):
                        sp.dma_start(raw[:, p, :], w8[p]).then_inc(raw_landed[p], 16)
            sp.wait_ge(x_turned, 8)
            sp.dma_start(cosb, cos).then_inc(rope_landed, 16)
            sp.dma_start(sinb, sin).then_inc(rope_landed, 16)

            with sp.Fori(1, T_MA // 2) as i:
                for p in range(2):
                    sp.wait_ge(lo_made, 2 * i + (p - 1))
                    sp.dma_start(raw[:, p, :], w8[2 * i + p]).then_inc(raw_landed[p], 16)

            def merge_loads(sp, i, t0, w8_0, up0):
                sp.wait_ge(lo_made, 2 * i + (split_index(t0) - 1))
                sp.dma_start(raw[:, 0, :], w8[i + w8_0]).then_inc(raw_landed[0], 16)
                sp.wait_ge(lo_made, 2 * i + split_index(t0))
                sp.dma_start(raw[:, 1, 0:AW], wup[i + up0]).then_inc(raw_landed[1], 16)

            with sp.Fori(0, KC) as i:
                merge_loads(sp, i, T_MA, T_MA, 0)
            n8 = T_MA + KC
            with sp.Fori(0, AC) as i:
                for p in range(2):
                    sp.wait_ge(lo_made, 2 * i + (T_ZB + p - 1))
                    sp.dma_start(raw[:, p, :], w8[2 * i + (n8 + p)]).then_inc(raw_landed[p], 16)
            n8 += 2 * AC
            sp.wait_ge(pv_done, 2 * NB)
            for b in range(2):
                sp.dma_start(memx[:, b, :], mem[b * P:(b + 1) * P, :]).then_inc(mem_landed, 16)
            for m in range(2):
                sp.wait_ge(lo_made, split_index(T_MQ + AC - 2) + m + 1)
                sp.dma_start(raw[:, m, :], wmem[m]).then_inc(raw_landed[m], 16)
            with sp.Fori(1, MHEADS) as i:
                for p in range(2):
                    sp.wait_ge(tile_done, 2 * i + (T_MEM + p - 1))
                    sp.dma_start(raw[:, p, :], wmem[2 * i + p]).then_inc(raw_landed[p], 16)
            sp.wait_ge(tile_done, T_MB - 1)
            sp.dma_start(raw[:, 0, :], w8[n8]).then_inc(raw_landed[0], 16)
            sp.wait_ge(tile_done, T_MB)
            sp.dma_start(raw[:, 1, 0:AW], wup[KC]).then_inc(raw_landed[1], 16)
            with sp.Fori(1, KC) as i:
                merge_loads(sp, i, T_MB, n8, KC)
            n8 += KC
            with sp.Fori(0, AC // 2) as i:
                for p in range(2):
                    sp.wait_ge(lo_made, 2 * i + (split_index(T_ZM) + p - 1))
                    sp.dma_start(raw[:, p, :], w8[2 * i + (n8 + p)]).then_inc(raw_landed[p], 16)
            n8 += AC
            with sp.Fori(0, KC) as i:
                merge_loads(sp, i, T_MM, n8, 2 * KC)
            sp.wait_ge(y_ready, 3 * AC)
            for n in range(2):
                sp.dma_start(wout_raw[:, n * KC * HALF:(n + 1) * KC * HALF], wout[n]).then_inc(wout_landed[n], 16)
            sp.dma_start(gpostb, g_post).then_inc(gpost_landed, 16)
            sp.wait_ge(lo_made, split_index(T_OUT))
            for p in range(2):
                sp.dma_start(raw[:, p, :], x[p * P:(p + 1) * P, :]).then_inc(xres_landed[p], 16)
            with sp.Fori(0, NB // 2 - 1) as i:
                for p in range(2):
                    sp.wait_ge(out_ready, 2 * i + (p + 1))
                    sp.dma_start(out[bass.ds((2 * i + p) * P, P), :], tout[:, p, :]).then_inc(stored[p], 16)
                    sp.dma_start(raw[:, p, :], x[bass.ds((2 * i + (p + 2)) * P, P), :]).then_inc(xres_landed[p], 16)
            for b in range(NB - 2, NB):
                sp.wait_ge(out_ready, b + 1)
                sp.dma_start(out[b * P:(b + 1) * P, :], tout[:, b % 2, :]).then_inc(stored[b % 2], 16)
            for p in range(2):
                sp.wait_ge(stored[p], 16 * (NB // 2))

        @block.gpsimd
        def _(pool):
            def low_part(p, nth):
                pool.wait_ge(hi_made, nth)
                nc.gpsimd.tensor_tensor(w_lo[:, p, :], raw[:, p, :], w_hi[:, p, :].bitcast(F32),
                                        ALU.subtract).then_inc(lo_made, 1)

            pool.wait_ge(x_turned, 8)
            nc.gpsimd.memset(q_swap, 0.0).then_inc(rope_landed, 16)
            with pool.Fori(0, split_index(T_OUT) // 2) as i:
                for p in range(2):
                    low_part(p, 2 * i + (p + 1))

        @block.tensor
        def _(pe):
            def product(t_half, p, chunks, src_hi, src_lo, nth, ready=None):
                await_count(pe, drained[p], t_half)
                pe.wait_ge(hi_made, nth)
                pe.wait_ge(lo_made, nth)
                for half in range(2):
                    if ready is not None:
                        ready(half)
                    cols = slice(half * HALF, (half + 1) * HALF)
                    for k in range(chunks):
                        hi, lo = w_hi[:, p, k * P:(k + 1) * P], w_lo[:, p, k * P:(k + 1) * P]
                        pe.matmul(pm[:, p, cols], hi, src_hi[:, k, cols], start=(k == 0), stop=False)
                        pe.matmul(pm[:, p, cols], hi, src_lo[:, k, cols], start=False, stop=False)
                        mm = pe.matmul(pm[:, p, cols], lo, src_hi[:, k, cols], start=False,
                                       stop=(k == chunks - 1))
                mm.then_inc(tile_done, 1)

            def from_h(i, t0, q=0, ready=None):
                at = (t0 + q) // 2 + i
                product(at, q % 2, KC, h_hi, h_lo, 2 * i + (split_index(t0) + q + 1), ready)

            def from_y(i, t0):
                product(t0 // 2 + i, 1, AC, y_hi, y_lo, 2 * i + (split_index(t0) + 2))

            pe.wait_ge(small_landed, 96)
            spare = [sa[:, 0, :], sa[:, 1, :], sa[:, 2, :], pv[:, :]]
            for n in range(2 * KC):
                half, k = divmod(n, KC)
                if k == 0:
                    pe.wait_ge(xs_made, half + 1)
                if n >= 4:
                    pe.wait_ge(h_made, n - 3)
                for b in range(4):
                    src = area_m[:, (4 * half + b) * D + k * P:(4 * half + b) * D + (k + 1) * P]
                    mm = pe.transpose(spare[n % 4][:, b * P:(b + 1) * P], src, ident[:, :])
                mm.then_inc(x_turned, 1)

            for q in range(2 + AC):
                p = q % 2
                if q < 2:
                    pe.wait_ge(hi_made, q + 1)
                ready = (lambda half: pe.wait_ge(h_made, KC * (half + 1))) if q == 0 else None
                from_h(0, T_QKV, q, ready)
                if q == 2:
                    pe.wait_ge(drained[1], 1)
                    for n in range(2):
                        for b in range(4):
                            mm = pe.transpose(sa[:, n, b * P:(b + 1) * P],
                                              vT[:, (4 * n + b) * P:(4 * n + b + 1) * P], ident[:, :])
                        mm.then_inc(v_turned, 1)

            with pe.Fori(0, AC) as j:
                for q in range(4):
                    product(2 * j + (T_CONV + q) // 2, q % 2, KC, h_hi, h_lo, 4 * j + (T_CONV + q + 1))

            def scores(i, g, window):
                if g == 0:
                    pe.wait_ge(q_staged, i + 1)
                for h in range(GROUP):
                    b = h % 2
                    if h < 2:
                        await_count(pe, pt_dve, 2 * i + g)
                        await_count(pe, pt_act, 4 * i + 2 * g)
                        pe.wait_ge(v_made, 2)
                    else:
                        pe.wait_ge(masked, 8 * i + (4 * g + h - 1))
                    pe.matmul(sa[:, b, 0:WIN], qz[:, g, h, :], window, start=True, stop=True).then_inc(scored, 1)

            def turn_probs(i, g):
                pe.wait_ge(p_ready, 2 * i + (g + 1))
                for j, bank in enumerate((2, 0, 1)):
                    for h in range(GROUP):
                        mm = pe.transpose(sa[:, bank, h * P:(h + 1) * P], probs[:, h, j * P:(j + 1) * P], ident[:, :])
                    mm.then_inc(turned, 1)

            def values(i, g):
                if g == 0:
                    pe.wait_ge(v_staged, i + 1)
                    await_count(pe, o_taken, i)
                for j in range(3):
                    if j == 1:
                        pe.wait_ge(pt_dve, 2 * i + (g + 1))
                    else:
                        pe.wait_ge(pt_act, 4 * i + (2 * g + 1 + j // 2))
                    mm = pe.matmul(pv[:, :], vwin[:, j, g, :], probsT[:, j, :, :].rearrange("p h q -> p (h q)"),
                                   start=(g == 0 and j == 0), stop=(g == 1 and j == 2))
                mm.then_inc(pv_done, 1)

            def merge_a(i, window, first=False):
                def attention_head():
                    scores(i, 0, window)
                    if not first:
                        values(i - 1, 1)
                if not first:
                    attention_head()
                from_h(i, T_MA)
                if first:
                    attention_head()
                turn_probs(i, 0)
                scores(i, 1, window)
                values(i, 0)
                if first:
                    pe.wait_ge(y_ready, AC)
                from_y(i, T_MA)
                turn_probs(i, 1)

            merge_a(0, kT[:, 0:WIN], first=True)
            with pe.Fori(1, NB - 1) as i:
                merge_a(i, kT[:, bass.ds((i - 1) * P, WIN)])
            merge_a(NB - 1, kT[:, SEQ - WIN:SEQ])
            values(NB - 1, 1)

            with pe.Fori(0, AC) as i:
                for q in range(2):
                    from_h(i, T_ZB, q)

            pe.wait_ge(memx_ready, 1)
            for n in range(4):
                if n >= 2:
                    pe.wait_ge(mn_made, n - 1)
                for kk in range(2):
                    for b in range(2):
                        k = 2 * n + kk
                        mm = pe.transpose(sa[:, n % 2, kk * MEM + b * P:kk * MEM + (b + 1) * P],
                                          memx[:, b, k * P:(k + 1) * P], ident[:, :])
                mm.then_inc(mem_turned, 1)
            pe.wait_ge(mn_made, 4)
            for n in range(2 * MHEADS):
                p, t = n % 2, T_MEM + n
                pe.wait_ge(drained[p], t // 2)
                pe.wait_ge(raw_landed[p], 16 * (t // 2 + 1))
                if n < MHEADS:
                    for k in range(KC):
                        mm = pe.matmul(pm[:, p, 0:MEM], raw[:, p, k * P:(k + 1) * P], mnT[:, k, :],
                                       start=(k == 0), stop=(k == KC - 1))
                else:
                    for b in range(2):
                        for k in range(KC):
                            mm = pe.matmul(pm[:, p, b * P:(b + 1) * P], mnT[:, k, b * P:(b + 1) * P],
                                           raw[:, p, k * P:(k + 1) * P], start=(k == 0), stop=(k == KC - 1))
                mm.then_inc(tile_done, 1)

            with pe.Fori(0, KC) as i:
                pe.wait_ge(mq_staged, i + 1)
                pe.wait_ge(drained[1], (T_MEM + 8) // 2)
                for b in range(2):
                    pe.wait_ge(*((pt_act, i + 4 * NB), (pt_dve, i + 2 * NB))[b])
                    for h in range(2 * b, 2 * b + 2):
                        mm = pe.matmul(sa[:, b, (h % 2) * MEM:(h % 2 + 1) * MEM], mqz[:, h, :], mkT[:, h, :],
                                       start=True, stop=True)
                    mm.then_inc(mscored, 1)
                from_h(i, T_MB)
                pe.wait_ge(mp_ready, i + 1)
                for b in range(2):
                    for h in range(MHEADS):
                        mm = pe.transpose(sa[:, b, h * P:(h + 1) * P], mprobs[:, h, b * P:(b + 1) * P], ident[:, :])
                    mm.then_inc(mturned, 1)
                pe.wait_ge(y_ready, 2 * AC)
                from_y(i, T_MB)
                pe.wait_ge(pt_act, i + (4 * NB + 1))
                pe.wait_ge(pt_dve, i + (2 * NB + 1))
                pe.wait_ge(o_taken, i + NB)
                for h in range(MHEADS):
                    for b in range(2):
                        mm = pe.matmul(pv[:, h * P:(h + 1) * P], mv[:, b, h * P:(h + 1) * P], mprobsT[:, b, h, :],
                                       start=(b == 0), stop=(b == 1))
                mm.then_inc(pv_done, 1)

            with pe.Fori(0, AC // 2) as i:
                for q in range(2):
                    from_h(i, T_ZM, q)
            with pe.Fori(0, KC) as i:
                from_h(i, T_MM)
                pe.wait_ge(y_ready, 3 * AC)
                from_y(i, T_MM)

            def out_block(i, p, first=False):
                b_no = 2 * i + p
                pe.wait_ge(drained[p], T_OUT // 2 + i)
                pe.wait_ge(mb_hi_made, b_no + 1)
                pe.wait_ge(mb_lo_made, b_no + 1)
                for half in range(2):
                    for k in range(KC):
                        if first:
                            pe.wait_ge(wo_lo_made, half * KC + k + 1)
                        n = half * KC + k
                        hi = mb_hi[:, (p * KC + k) * P:(p * KC + k + 1) * P]
                        lo = mb_lo[:, (p * KC + k) * P:(p * KC + k + 1) * P]
                        dst = pm[:, p, half * HALF:(half + 1) * HALF]
                        pe.matmul(dst, hi, wo_hi[:, n * HALF:(n + 1) * HALF], start=(k == 0), stop=False)
                        pe.matmul(dst, lo, wo_hi[:, n * HALF:(n + 1) * HALF], start=False, stop=False)
                        mm = pe.matmul(dst, hi, wo_lo[:, n * HALF:(n + 1) * HALF], start=False, stop=(k == KC - 1))
                mm.then_inc(tile_done, 1)

            out_block(0, 0, first=True)
            out_block(0, 1)
            with pe.Fori(1, NB // 2) as i:
                for p in range(2):
                    out_block(i, p)

        @block.scalar
        def _(act):
            def split_next(p, t_half, nth):
                act.wait_ge(raw_landed[p], 16 * t_half + 16)
                nc.scalar.activation(w_hi[:, p, :], raw[:, p, :], ACT.Copy).then_inc(hi_made, 1)

            def after_tile(t0, per, i, p):
                act.wait_ge(tile_done, per * i + (t0 + 1))
                split_next(p, (per // 2) * i + (t0 + 2) // 2, per * i + (split_index(t0) + 3))

            for b in range(0, NB, 2):
                act.wait_ge(x_landed[b], 16)
                nc.scalar.activation(area_a[:, (b // 2) * D:(b // 2 + 1) * D], area_m[:, b * D:(b + 1) * D],
                                     ACT.Square, accum_out=st[:, 0, b:b + 1]).then_inc(ssq_act, 1)
                if b % 4 == 2:
                    half = b // 4
                    if half == 0:
                        split_next(0, 0, 1)
                        split_next(1, 0, 2)
                    act.wait_ge(var_made, half + 1)
                    nc.scalar.activation(st[:, 2, 4 * half:4 * half + 4], st[:, 1, 4 * half:4 * half + 4],
                                         ACT.Sqrt).then_inc(root_made, 1)
            act.wait_ge(small_landed, 96)
            for n in range(2 * KC):
                half, k = divmod(n, KC)
                bank = [sa[:, 0, :], sa[:, 1, :], sa[:, 2, :], pv[:, :]][n % 4]
                act.wait_ge(x_turned, n + 1)
                nc.scalar.activation(h_hi[:, k, half * HALF:(half + 1) * HALF], bank, ACT.Identity,
                                     scale=gpre[:, k:k + 1]).then_inc(h_hi_made, 1)

            act.wait_ge(h_made, 2 * KC)
            for q in range(2 + AC):
                p = q % 2
                act.wait_ge(tile_done, q + 1)
                if q == 1:
                    nc.scalar.copy(vT, pm[:, 1, :]).then_inc(drained[1], 1)
                else:
                    n = q if q == 0 else q - 1
                    if n:
                        act.wait_ge(roped, n)
                    else:
                        act.wait_ge(rope_landed, 48)
                    nc.scalar.copy(q_raw, pm[:, p, :]).then_inc(drained[p], 1)
                    act.wait_ge(drained[p], q // 2 + 1)
                    for row in (0, HEAD):
                        half_rot = ROT // 2
                        act.dma_start(q_swap[row:row + half_rot, :],
                                      q_raw[row + half_rot:row + ROT, :]).then_inc(swapped, 16)
                        act.dma_start(q_swap[row + half_rot:row + ROT, :],
                                      q_raw[row:row + half_rot, :]).then_inc(swapped, 16)
                split_next(p, (q + 2) // 2, q + 3)
                if q == 2:
                    for n in range(2):
                        act.wait_ge(v_turned, n + 1)
                        nc.scalar.copy(vtok[:, 4 * n:4 * n + 4, :],
                                       sa[:, n, :].rearrange("p (b d) -> p b d", b=4)).then_inc(v_made, 1)

            with act.Fori(0, AC) as j:
                act.wait_ge(tile_done, 4 * j + (T_CONV + 1))
                act.wait_ge(drained[1], 2 * j + T_CONV // 2)
                nc.scalar.copy(conv_c, pm[:, 0, :]).then_inc(drained[0], 1)
                split_next(0, 2 * j + (T_CONV + 2) // 2, 4 * j + (T_CONV + 3))
                after_tile(T_CONV + 1, 4, j, 1)
                after_tile(T_CONV + 2, 4, j, 0)
                act.wait_ge(tile_done, 4 * j + (T_CONV + 4))
                act.wait_ge(drained[1], 2 * j + (T_CONV // 2 + 1))
                nc.scalar.activation(sig, pm[:, 1, :], ACT.Sigmoid).then_inc(sig_made, 1)
                split_next(1, 2 * j + (T_CONV + 5) // 2, 4 * j + (T_CONV + 6))
                act.wait_ge(y_made, j + 1)
                nc.scalar.activation(y_hi[:, j, :], sig, ACT.Copy).then_inc(y_hi_made, 1)

            def exps(i, g):
                act.wait_ge(nm_ready, 2 * i + (g + 1))
                nc.scalar.activation(st[:, 4, 4:8], st[:, 4, 0:4], ACT.Exp)
                for h in range(GROUP):
                    ins = nc.scalar.activation(probs[:, h, :], probs[:, h, :], ACT.Exp,
                                               bias=st[:, 3, h:h + 1], accum_out=st[:, 5, h:h + 1])
                ins.then_inc(exped, 1)

            def take_probs(i, g):
                await_count(act, pv_done, 2 * i + g)
                for n, (j, bank) in enumerate(((0, 2), (2, 1))):
                    act.wait_ge(turned, 6 * i + (3 * g + j + 1))
                    nc.scalar.copy(probsT[:, j, :, :],
                                   sa[:, bank, :].rearrange("p (h q) -> p h q", h=GROUP)).then_inc(pt_act, 1)

            def merge_a(i):
                exps(i, 0)
                act.wait_ge(tile_done, 2 * i + (T_MA + 1))
                act.wait_ge(drained[1], i + T_MA // 2)
                nc.scalar.activation(sig, pm[:, 0, :], ACT.Sigmoid).then_inc(drained[0], 1)
                split_next(0, i + (T_MA + 2) // 2, 2 * i + (T_MA + 3))
                take_probs(i, 0)
                exps(i, 1)
                act.wait_ge(tile_done, 2 * i + (T_MA + 2))
                split_next(1, i + (T_MA + 2) // 2, 2 * i + (T_MA + 4))
                take_probs(i, 1)

            act.wait_ge(y_ready, AC)
            merge_a(0)
            with act.Fori(1, NB) as i:
                merge_a(i)

            def gated(i, q, t0, n0):
                p = q
                act.wait_ge(tile_done, 2 * i + (t0 + q + 1))
                act.wait_ge(y_ready, 2 * i + (n0 + q))
                nc.scalar.activation(sig, pm[:, p, :], ACT.Sigmoid).then_inc(sig_made, 1)
                split_next(p, i + (t0 + q + 2) // 2, 2 * i + (split_index(t0) + q + 3))
                act.wait_ge(y_made, 2 * i + (n0 + q + 1))
                nc.scalar.activation(y_hi[:, 2 * i + q, :], sig, ACT.Copy).then_inc(y_hi_made, 1)

            act.wait_ge(drained[1], T_ZB // 2)
            with act.Fori(0, AC // 2) as i:
                for q in range(2):
                    gated(i, q, T_ZB, AC)
            for q in range(2):
                after_tile(T_MQ + q, 2, 0, q)
            act.wait_ge(var_made, 3)
            nc.scalar.activation(st[:, 2, 0:2], st[:, 1, 0:2], ACT.Sqrt).then_inc(root_made, 1)
            for n in range(2 * MHEADS):
                p, t = n % 2, T_MEM + n
                act.wait_ge(tile_done, t + 1)
                if n < MHEADS:
                    nc.scalar.copy(mkT[:, n, :], pm[:, p, 0:MEM]).then_inc(drained[p], 1)
                else:
                    nc.scalar.copy(mv[:, :, (n - MHEADS) * P:(n - MHEADS + 1) * P],
                                   pm[:, p, 0:MEM].rearrange("p (b d) -> p b d", b=2)).then_inc(drained[p], 1)
            for p in range(2):
                split_next(p, (T_MB + p) // 2, split_index(T_MB) + p + 1)

            act.wait_ge(y_ready, 2 * AC)
            with act.Fori(0, KC) as i:
                act.wait_ge(mnm_ready, i + 1)
                for h in range(MHEADS):
                    ins = nc.scalar.activation(mprobs[:, h, :], sa[:, h // 2, (h % 2) * MEM:(h % 2 + 1) * MEM],
                                               ACT.Exp, bias=st[:, 3, h:h + 1], scale=float(P) ** -0.5,
                                               accum_out=st[:, 5, h:h + 1])
                ins.then_inc(mexped, 1)
                act.wait_ge(tile_done, 2 * i + (T_MB + 1))
                nc.scalar.activation(sig, pm[:, 0, :], ACT.Sigmoid).then_inc(drained[0], 1)
                split_next(0, i + (T_MB + 2) // 2, 2 * i + (split_index(T_MB) + 3))
                act.wait_ge(mturned, 2 * i + 1)
                act.wait_ge(pv_done, i + 2 * NB)
                nc.scalar.copy(mprobsT[:, 0, :, :],
                               sa[:, 0, :].rearrange("p (h q) -> p h q", h=MHEADS)).then_inc(pt_act, 1)
                act.wait_ge(tile_done, 2 * i + (T_MB + 2))
                split_next(1, i + (T_MB + 2) // 2, 2 * i + (split_index(T_MB) + 4))

            act.wait_ge(merged_done, KC)
            with act.Fori(0, AC // 2) as i:
                for q in range(2):
                    gated(i, q, T_ZM, 2 * AC)

            def gate_m(i, more):
                act.wait_ge(tile_done, 2 * i + (T_MM + 1))
                act.wait_ge(merged_done, i + KC)
                nc.scalar.activation(sig, pm[:, 0, :], ACT.Sigmoid).then_inc(drained[0], 1)
                if more:
                    split_next(0, i + (T_MM + 2) // 2, 2 * i + (split_index(T_MM) + 3))
                    act.wait_ge(tile_done, 2 * i + (T_MM + 2))
                    split_next(1, i + (T_MM + 2) // 2, 2 * i + (split_index(T_MM) + 4))

            act.wait_ge(y_ready, 3 * AC)
            with act.Fori(0, KC - 1) as i:
                gate_m(i, True)
            gate_m(KC - 1, False)

            def wout_high(half):
                act.wait_ge(wout_landed[half], 16)
                for k in range(KC):
                    n = half * KC + k
                    nc.scalar.activation(wo_hi[:, n * HALF:(n + 1) * HALF], wout_raw[:, n * HALF:(n + 1) * HALF],
                                         ACT.Copy).then_inc(wo_hi_made, 1)

            def merged_high(p, at):
                nc.scalar.activation(mb_hi[:, p * D:(p + 1) * D].rearrange("p (k q) -> p k q", k=KC), at,
                                     ACT.Copy).then_inc(mb_hi_made, 1)

            wout_high(0)
            act.wait_ge(merged_done, 2 * KC)
            for b in range(2):
                merged_high(b, merged[:, :, b * P:(b + 1) * P])
                if b == 0:
                    wout_high(1)

            def out_block(i, p, more):
                act.wait_ge(tile_done, 2 * i + (T_OUT + p + 1))
                await_count(act, stored[p], 16 * i)
                nc.scalar.activation(tout[:, p, :], pm[:, p, :], ACT.Square,
                                     accum_out=st[:, 6, p:p + 1]).then_inc(sq_made, 1)
                if more:
                    merged_high(p, merged[:, :, bass.ds((2 * i + (p + 2)) * P, P)])
                act.wait_ge(out_var, 2 * i + (p + 1))
                nc.scalar.activation(st[:, 8, p:p + 1], st[:, 7, p:p + 1], ACT.Sqrt).then_inc(out_root, 1)

            for p in range(2):
                out_block(0, p, True)
            with act.Fori(1, NB // 2 - 1) as i:
                for p in range(2):
                    out_block(i, p, True)
            for p in range(2):
                out_block(NB // 2 - 1, p, False)

        @block.vector
        def _(dve):
            chain = Chain(dve, dve_chain)
            link = chain.link

            def inv_root(var, root, r, t):
                link(nc.vector.reciprocal(r, root))
                link(nc.vector.tensor_tensor(t, r, r, ALU.mult))
                link(nc.vector.tensor_tensor(t, t, var, ALU.mult))
                link(nc.vector.tensor_scalar(t, t, -0.5, 1.5, ALU.mult, ALU.add))
                link(nc.vector.tensor_tensor(r, r, t, ALU.mult))

            for half in range(2):
                for b in (4 * half + 1, 4 * half + 3):
                    dve.wait_ge(x_landed[b], 16)
                    link(nc.vector.tensor_tensor_reduce(
                        out=area_a[:, (4 + b // 2) * D:(5 + b // 2) * D], in0=area_m[:, b * D:(b + 1) * D],
                        in1=area_m[:, b * D:(b + 1) * D], scale=1.0, scalar=0.0, op0=ALU.mult, op1=ALU.add,
                        accum_out=st[:, 0, b:b + 1]))
                dve.wait_ge(ssq_act, 2 * half + 2)
                cols = slice(4 * half, 4 * half + 4)
                nc.vector.tensor_scalar(st[:, 1, cols], st[:, 0, cols], 1.0 / D, EPS, ALU.mult,
                                        ALU.add).then_inc(var_made, 1)
                dve.wait_ge(var_made, half + 1)
                dve.wait_ge(root_made, half + 1)
                inv_root(st[:, 1, cols], st[:, 2, cols], st[:, 9, cols], st[:, 10, cols])
                for b in range(4 * half, 4 * half + 4):
                    if b % 2 == 0:
                        dve.wait_ge(x_landed[b], 16)
                    ins = nc.vector.tensor_scalar(area_m[:, b * D:(b + 1) * D], area_m[:, b * D:(b + 1) * D],
                                                  st[:, 9, b:b + 1], None, ALU.mult)
                ins.then_inc(xs_made, 1)
            dve.wait_ge(small_landed, 96)
            for n in range(2 * KC):
                half, k = divmod(n, KC)
                cols = slice(half * HALF, (half + 1) * HALF)
                bank = [sa[:, 0, :], sa[:, 1, :], sa[:, 2, :], pv[:, :]][n % 4]
                dve.wait_ge(h_hi_made, n + 1)
                nc.vector.scalar_tensor_tensor(out=h_lo[:, k, cols], in0=bank, scalar=gpre[:, k:k + 1],
                                               in1=h_hi[:, k, cols].bitcast(F32), op0=ALU.mult,
                                               op1=ALU.subtract).then_inc(h_made, 1)

            dve.wait_ge(rope_landed, 48)
            for n in range(1 + AC):
                dst = kT if n == 0 else qT[:, n - 1, :]
                dve.wait_ge(drained[0 if n == 0 else (n + 1) % 2], 1 if n == 0 else (n + 1) // 2 + 1)
                link(nc.vector.tensor_tensor(dst, q_raw, cosb, ALU.mult))
                dve.wait_ge(swapped, 64 * (n + 1))
                link(nc.vector.tensor_tensor(rot_t, q_swap, sinb, ALU.mult))
                nc.vector.tensor_tensor(dst, dst, rot_t, ALU.add).then_inc(roped, 1)

            nc.vector.memset(conv_cu[:, 0:1], 0.0)
            link(nc.vector.memset(conv_cu[:, SEQ + 1:SEQ + 2], 0.0))
            with chain.loop(0, AC, 3) as j:
                dve.wait_ge(tile_done, 4 * j + (T_CONV + 2))
                dve.wait_ge(drained[0], 2 * j + (T_CONV // 2 + 1))
                nc.vector.tensor_tensor(conv_cu[:, 1:SEQ + 1], pm[:, 1, :], conv_c, ALU.mult).then_inc(drained[1], 1)
                dve.wait_ge(drained[1], 2 * j + (T_CONV // 2 + 1))
                link(nc.vector.tensor_scalar(conv_t, conv_cu[:, 0:SEQ], wconv[:, 0, bass.ds(j, 1)], None, ALU.mult))
                for tap in (1, 2):
                    link(nc.vector.scalar_tensor_tensor(out=conv_t, in0=conv_cu[:, tap:tap + SEQ],
                                                        scalar=wconv[:, tap, bass.ds(j, 1)], in1=conv_t,
                                                        op0=ALU.mult, op1=ALU.add))
                dve.wait_ge(tile_done, 4 * j + (T_CONV + 3))
                nc.vector.tensor_tensor(conv_t, pm[:, 0, :], conv_t, ALU.mult).then_inc(drained[0], 1)
                dve.wait_ge(sig_made, j + 1)
                dve.wait_ge(drained[0], 2 * j + (T_CONV // 2 + 2))
                nc.vector.tensor_tensor(sig, pm[:, 1, :], sig, ALU.mult).then_inc(drained[1], 1)
                dve.wait_ge(drained[1], 2 * j + (T_CONV // 2 + 2))
                nc.vector.tensor_tensor(sig, conv_t, sig, ALU.mult).then_inc(y_made, 1)
                dve.wait_ge(y_hi_made, j + 1)
                nc.vector.tensor_tensor(y_lo[:, j, :], sig, y_hi[:, j, :].bitcast(F32),
                                        ALU.subtract).then_inc(y_ready, 1)
                dve.wait_ge(y_ready, j + 1)

            nc.vector.memset(qz[HEAD:P, 0, :, :], 0.0)
            nc.vector.memset(qz[0:HEAD, 1, :, :], 0.0)
            nc.vector.memset(vwin[:, :, 0, HEAD:P], 0.0)
            link(nc.vector.memset(vwin[:, :, 1, 0:HEAD], 0.0))

            def stage_q(at):
                link(nc.vector.tensor_copy(qz[0:HEAD, 0, :, :], qT[0:HEAD, :, at]))
                nc.vector.tensor_copy(qz[HEAD:P, 1, :, :], qT[HEAD:P, :, at]).then_inc(q_staged, 1)

            def softmax_head(i, g, mask_at):
                for h in range(GROUP):
                    dve.wait_ge(scored, 8 * i + (4 * g + h + 1))
                    nc.vector.memset(st[:, 11, GROUP * g + h:GROUP * g + h + 1], 0.0)
                    nc.vector.tensor_tensor_reduce(
                        out=probs[:, h, :], in0=sa[:, h % 2, 0:WIN], in1=maskb[:, mask_at:mask_at + WIN],
                        scale=float(HEAD) ** -0.5, scalar=-3.0e38, op0=ALU.add, op1=ALU.max,
                        accum_out=st[:, 0, h:h + 1]).then_inc(masked, 1)
                dve.wait_ge(masked, 8 * i + (4 * g + 4))
                sinks = sinkb[:, GROUP * g:GROUP * g + GROUP]
                link(nc.vector.tensor_tensor(st[:, 1, 0:4], st[:, 0, 0:4], sinks, ALU.max))
                link(nc.vector.tensor_scalar(st[:, 3, 0:4], st[:, 1, 0:4], -1.0, None, ALU.mult))
                nc.vector.tensor_tensor(st[:, 4, 0:4], sinks, st[:, 3, 0:4], ALU.add).then_inc(nm_ready, 1)

            def softmax_tail(i, g):
                dve.wait_ge(exped, 2 * i + (g + 1))
                link(nc.vector.tensor_tensor(st[:, 5, 4:8], st[:, 5, 0:4], st[:, 4, 4:8], ALU.add))
                link(nc.vector.reciprocal(st[:, 6, 0:4], st[:, 5, 4:8]))
                for h in range(GROUP):
                    ins = nc.vector.tensor_scalar(probs[:, h, :], probs[:, h, :], st[:, 6, h:h + 1], None, ALU.mult)
                ins.then_inc(p_ready, 1)

            def take_probs(i, g):
                dve.wait_ge(turned, 6 * i + (3 * g + 2))
                await_count(dve, pv_done, 2 * i + g)
                nc.vector.tensor_copy(probsT[:, 1, :, :],
                                      sa[:, 0, :].rearrange("p (h q) -> p h q", h=GROUP)).then_inc(pt_dve, 1)

            def take_output(i, at):
                dve.wait_ge(pv_done, 2 * i + 2)
                nc.vector.tensor_copy(qT[:, :, at], pv[:, :].rearrange("p (c q) -> p c q", c=AC)).then_inc(o_taken, 1)

            def merge_a(i, window, mask_at, before, after):
                softmax_head(i, 0, mask_at)
                if before is not None:
                    take_output(i - 1, before)
                link(nc.vector.tensor_copy(vwin[:, :, 0, 0:HEAD], vtok[:, window, 0:HEAD]))
                nc.vector.tensor_copy(vwin[:, :, 1, HEAD:P], vtok[:, window, HEAD:P]).then_inc(v_staged, 1)
                softmax_tail(i, 0)
                take_probs(i, 0)
                softmax_head(i, 1, mask_at)
                softmax_tail(i, 1)
                if after is not None:
                    stage_q(after)
                dve.wait_ge(tile_done, 2 * i + (T_MA + 2))
                dve.wait_ge(drained[0], i + (T_MA // 2 + 1))
                at = i if isinstance(i, int) else bass.ds(i, 1)
                nc.vector.tensor_tensor(merged[:, at, :], sig, pm[:, 1, :], ALU.mult).then_inc(drained[1], 1)
                take_probs(i, 1)

            LINKS_A = 10
            stage_q(slice(0, P))
            merge_a(0, slice(0, 3), 2 * P, None, slice(P, 2 * P))
            with chain.loop(1, NB - 1, LINKS_A) as i:
                merge_a(i, bass.ds(i - 1, 3), P, bass.ds((i - 1) * P, P), bass.ds((i + 1) * P, P))
            merge_a(NB - 1, slice(NB - 3, NB), 0, slice((NB - 2) * P, (NB - 1) * P), None)
            take_output(NB - 1, slice((NB - 1) * P, SEQ))
            dve.wait_ge(o_taken, NB)

            def gated(i, q, t0, n0):
                p = q
                dve.wait_ge(sig_made, 2 * i + (n0 + q + 1))
                nc.vector.tensor_tensor(sig, pm[:, p, :], sig, ALU.mult).then_inc(drained[p], 1)
                dve.wait_ge(drained[p], i + ((t0 + q) // 2 + 1))
                at = bass.ds(2 * i + q, 1)
                nc.vector.tensor_tensor(sig, qT[:, at, :], sig, ALU.mult).then_inc(y_made, 1)
                dve.wait_ge(y_hi_made, 2 * i + (n0 + q + 1))
                nc.vector.tensor_tensor(y_lo[:, at, :], sig, y_hi[:, at, :].bitcast(F32),
                                        ALU.subtract).then_inc(y_ready, 1)
                dve.wait_ge(y_ready, 2 * i + (n0 + q + 1))

            with dve.Fori(0, AC // 2) as i:
                for q in range(2):
                    gated(i, q, T_ZB, AC)
            with dve.Fori(0, AC // 2) as i:
                for q in range(2):
                    dve.wait_ge(tile_done, 2 * i + (T_MQ + q + 1))
                    nc.vector.tensor_copy(qT[:, bass.ds(2 * i + q, 1), :], pm[:, q, :]).then_inc(drained[q], 1)
                    dve.wait_ge(drained[q], i + ((T_MQ + q) // 2 + 1))

            dve.wait_ge(mem_landed, 32)
            for b in range(2):
                link(nc.vector.tensor_tensor_reduce(out=mnT[:, 4 * b:4 * b + 4, :], in0=memx[:, b, :],
                                                    in1=memx[:, b, :], scale=1.0, scalar=0.0, op0=ALU.mult,
                                                    op1=ALU.add, accum_out=st[:, 0, b:b + 1]))
            nc.vector.tensor_scalar(st[:, 1, 0:2], st[:, 0, 0:2], 1.0 / D, EPS, ALU.mult, ALU.add).then_inc(var_made, 1)
            dve.wait_ge(var_made, 3)
            dve.wait_ge(root_made, 3)
            inv_root(st[:, 1, 0:2], st[:, 2, 0:2], st[:, 9, 0:2], st[:, 10, 0:2])
            for b in range(2):
                ins = nc.vector.tensor_scalar(memx[:, b, :], memx[:, b, :], st[:, 9, b:b + 1], None, ALU.mult)
            ins.then_inc(memx_ready, 1)
            for n in range(4):
                dve.wait_ge(mem_turned, n + 1)
                for kk in range(2):
                    k = 2 * n + kk
                    ins = nc.vector.tensor_scalar(mnT[:, k, :], sa[:, n % 2, kk * MEM:(kk + 1) * MEM],
                                                  gmem[:, k:k + 1], None, ALU.mult)
                ins.then_inc(mn_made, 1)

            def stage_mq(at):
                nc.vector.tensor_copy(mqz, qT[:, :, at]).then_inc(mq_staged, 1)

            def merge_in(i, t0, n0):
                dve.wait_ge(tile_done, 2 * i + (t0 + 2))
                dve.wait_ge(drained[0], i + (t0 // 2 + 1))
                nc.vector.tensor_tensor(sig, sig, pm[:, 1, :], ALU.mult).then_inc(drained[1], 1)
                dve.wait_ge(drained[1], i + (t0 // 2 + 1))
                at = i if isinstance(i, int) else bass.ds(i, 1)
                nc.vector.tensor_tensor(merged[:, at, :], merged[:, at, :], sig, ALU.add).then_inc(merged_done, 1)

            def merge_b(i, here, after):
                for b in range(2):
                    dve.wait_ge(mscored, 2 * i + (b + 1))
                    link(nc.vector.tensor_reduce(st[:, 0, 2 * b:2 * b + 2],
                                                 sa[:, b, :].rearrange("p (h m) -> p h m", h=2), AX.X, ALU.max))
                nc.vector.tensor_scalar(st[:, 3, 0:4], st[:, 0, 0:4], -float(P) ** -0.5, None,
                                        ALU.mult).then_inc(mnm_ready, 1)
                if after is not None:
                    stage_mq(after)
                dve.wait_ge(mexped, i + 1)
                link(nc.vector.reciprocal(st[:, 6, 0:4], st[:, 5, 0:4]))
                for h in range(MHEADS):
                    ins = nc.vector.tensor_scalar(mprobs[:, h, :], mprobs[:, h, :], st[:, 6, h:h + 1], None, ALU.mult)
                ins.then_inc(mp_ready, 1)
                dve.wait_ge(mturned, 2 * i + 2)
                dve.wait_ge(pv_done, i + 2 * NB)
                nc.vector.tensor_copy(mprobsT[:, 1, :, :],
                                      sa[:, 1, :].rearrange("p (h q) -> p h q", h=MHEADS)).then_inc(pt_dve, 1)
                merge_in(i, T_MB, 0)
                dve.wait_ge(pv_done, i + (2 * NB + 1))
                nc.vector.tensor_copy(qT[:, :, here], pv[:, :].rearrange("p (h q) -> p h q", h=MHEADS)).then_inc(o_taken, 1)

            LINKS_B = 3
            stage_mq(slice(0, P))
            with chain.loop(0, NB - 1, LINKS_B) as i:
                merge_b(i, bass.ds(i * P, P), bass.ds((i + 1) * P, P))
            merge_b(NB - 1, slice((NB - 1) * P, SEQ), None)
            dve.wait_ge(o_taken, 2 * NB)
            dve.wait_ge(merged_done, KC)

            with dve.Fori(0, AC // 2) as i:
                for q in range(2):
                    gated(i, q, T_ZM, 2 * AC)
            with dve.Fori(0, KC - 1) as i:
                merge_in(i, T_MM, KC)

            def wout_low(half):
                for k in range(KC):
                    n = half * KC + k
                    dve.wait_ge(wo_hi_made, n + 1)
                    nc.vector.tensor_tensor(wo_lo[:, n * HALF:(n + 1) * HALF], wout_raw[:, n * HALF:(n + 1) * HALF],
                                            wo_hi[:, n * HALF:(n + 1) * HALF].bitcast(F32),
                                            ALU.subtract).then_inc(wo_lo_made, 1)

            def merged_low(p, at, b1):
                dve.wait_ge(mb_hi_made, b1)
                nc.vector.tensor_tensor(mb_lo[:, p * D:(p + 1) * D].rearrange("p (k q) -> p k q", k=KC), at,
                                        mb_hi[:, p * D:(p + 1) * D].bitcast(F32).rearrange("p (k q) -> p k q", k=KC),
                                        ALU.subtract).then_inc(mb_lo_made, 1)

            wout_low(0)
            merge_in(KC - 1, T_MM, KC)
            merged_low(0, merged[:, :, 0:P], 1)
            wout_low(1)
            merged_low(1, merged[:, :, P:2 * P], 2)

            dve.wait_ge(gpost_landed, 16)

            def out_block(i, p, more):
                dve.wait_ge(sq_made, 2 * i + (p + 1))
                var, root, r, t = (st[:, n, p:p + 1] for n in (7, 8, 9, 10))
                nc.vector.tensor_scalar(var, st[:, 6, p:p + 1], 1.0 / D, EPS, ALU.mult, ALU.add).then_inc(out_var, 1)
                dve.wait_ge(out_var, 2 * i + (p + 1))
                if more:
                    merged_low(p, merged[:, :, bass.ds((2 * i + (p + 2)) * P, P)], 2 * i + (p + 3))
                dve.wait_ge(out_root, 2 * i + (p + 1))
                inv_root(var, root, r, t)
                nc.vector.scalar_tensor_tensor(out=tout[:, p, :], in0=pm[:, p, :], scalar=r, in1=gpostb,
                                               op0=ALU.mult, op1=ALU.mult).then_inc(drained[p], 1)
                dve.wait_ge(drained[p], i + (T_OUT // 2 + 1))
                dve.wait_ge(xres_landed[p], 16 * i + 16)
                nc.vector.tensor_tensor(tout[:, p, :], tout[:, p, :], raw[:, p, :], ALU.add).then_inc(out_ready, 1)

            with chain.loop(0, NB // 2 - 1, 10) as i:
                for p in range(2):
                    out_block(i, p, True)
            for p in range(2):
                out_block(NB // 2 - 1, p, False)


def _units(np_, w, order):
    rows = w.shape[0]
    u = w.reshape(rows // P, P, w.shape[1] // P, P)[:, :, order, :]
    return np_.ascontiguousarray(u.transpose(2, 1, 0, 3)).reshape(len(order), P, rows)


def _tables():
    half = ROT // 2
    inv = np.power(np.float64(ROPE_THETA), -np.arange(half) * (2.0 / ROT)).astype(np.float32)
    ang = (np.arange(SEQ, dtype=np.float32)[None, :] * inv[:, None]).astype(np.float64)
    cos, sin = np.ones((P, SEQ), np.float32), np.zeros((P, SEQ), np.float32)
    for row in (0, HEAD):
        cos[row:row + half] = cos[row + half:row + ROT] = np.cos(ang)
        sin[row:row + half], sin[row + half:row + ROT] = -np.sin(ang), np.sin(ang)
    q, k = np.arange(P)[:, None], np.arange(P)[None, :]
    none = np.full((P, P), -1e30, np.float32)
    left = np.where(k >= q, 0, none).astype(np.float32)
    right = np.where(k <= q, 0, none).astype(np.float32)
    strip = np.concatenate([none, left, np.zeros((P, P), np.float32), right, none], axis=1)
    return cos, sin, strip, np.eye(P, dtype=np.float32)


def kernel(x, mem, g_pre, w_in, w_conv, attn_sink, g_mem, w_mem_kv, w_up_a, w_up_b, w_up_m, w_out, g_post):
    import concourse.bacc as bacc
    from concourse.bass_utils import run_bass_kernel_spmd as run

    w_in = np.asarray(w_in)[0]
    pair = np.concatenate([np.r_[c * HEAD:(c + 1) * HEAD, (c + GROUP) * HEAD:(c + GROUP + 1) * HEAD]
                           for c in range(AC)])
    start = np.cumsum([0, AW, AW, AW, AW, AW, P, P, AW, AW, AW])
    a_b, a_c, a_x, a_z, b_q, b_k, b_v, b_z, m_q, m_z, gates = start
    cols = [np.arange(b_k, b_k + P), np.arange(b_v, b_v + P), b_q + pair]
    for c in range(AC):
        cols += [np.arange(s + c * P, s + (c + 1) * P) for s in (a_c, a_x, a_b, a_z)]
    cols += [np.arange(gates, gates + D), b_z + pair, np.arange(m_q, m_q + AW),
             np.arange(gates + D, gates + 2 * D), np.arange(m_z, m_z + AW),
             np.arange(gates + 2 * D, gates + 3 * D)]
    w8 = _units(np, w_in[:, np.concatenate(cols)], np.arange(w_in.shape[1] // P))
    wup = np.concatenate([_units(np, w, np.arange(KC)) for w in
                          (np.asarray(w_up_a)[0], np.asarray(w_up_b)[0][pair], np.asarray(w_up_m)[0])])
    wmem = _units(np, np.asarray(w_mem_kv)[0], np.arange(2 * MHEADS))
    wout = np.ascontiguousarray(np.asarray(w_out)[0].reshape(KC, P, 2, HALF).transpose(2, 1, 0, 3)
                                ).reshape(2, P, KC * HALF)
    cos, sin, strip, eye = _tables()

    def columns(g):
        return np.ascontiguousarray(np.asarray(g)[0].reshape(-1, P).T)

    arrays = {
        "x": np.asarray(x)[0], "mem": np.asarray(mem)[0], "w8": w8, "wup": wup, "wmem": wmem, "wout": wout,
        "g_pre": columns(g_pre), "g_mem": columns(g_mem),
        "g_post": np.ascontiguousarray(np.broadcast_to(np.asarray(g_post)[0], (P, D))),
        "w_conv": np.ascontiguousarray(np.asarray(w_conv)[0].reshape(3, AC, P).transpose(2, 0, 1)),
        "sink": np.ascontiguousarray(np.broadcast_to(np.asarray(attn_sink)[0], (P, HEADS))),
        "cos": cos, "sin": sin, "mask": strip, "ident": eye,
    }
    nc = bacc.Bacc("TRN2", target_bir_lowering=False, num_devices=1)
    ins = [nc.dram_tensor(f"in_{n}", a.shape, F32, kind="ExternalInput").ap() for n, a in arrays.items()]
    out = nc.dram_tensor("out_0", (SEQ, D), F32, kind="ExternalOutput").ap()
    hybrid_layer(nc, *ins, out)
    r = run(nc, [{f"in_{n}": np.ascontiguousarray(a) for n, a in arrays.items()}], core_ids=[0])
    return r.results[0]["out_0"].reshape(1, SEQ, D)
```

```python
from contextlib import ExitStack, contextmanager

import numpy as np

import concourse.bass as bass
from concourse import mybir

P = 128
D = 1024
SEQ = 1024
KC = D // P
NB = SEQ // P
HALF = 512
AW = D // 2
AC = AW // P
HEAD = 64
GROUP = 4
HEADS = 8
MEM = 256
MHEADS = 4
WIN = 3 * P
EPS = 1e-6
ROPE_THETA = 500000.0
ROT = HEAD // 4

F32 = mybir.dt.float32
F32R = mybir.dt.float32r
ALU = mybir.AluOpType
ACT = mybir.ActivationFunctionType
AX = mybir.AxisListType

T_QKV = 0
T_CONV = T_QKV + 2 + AC
T_MA = T_CONV + 4 * AC
T_ZB = T_MA + 2 * KC
T_MQ = T_ZB + AC
T_MEM = T_MQ + AC
T_MB = T_MEM + 2 * MHEADS
T_ZM = T_MB + 2 * KC
T_MM = T_ZM + AC
T_OUT = T_MM + 2 * KC

Q0, K0, V0, QZ0, P0, PT0, VW0, SIG0, AREA_A = 0, 4096, 5120, 6144, 7168, 8704, 10240, 11008, 12288
MK0, MV0, MX0, MNH0, MNL0 = 4096, 5120, 6144, 8192, 10240
MP0, MPT0, MPH0, MQZ0 = 6144, 7168, 8192, 9216
GP0, TO0 = 8192, 9216
QRAW0, SWAP0, COS0, SIN0, ROT0, VT0 = 0, 1024, 2048, 3072, 4096, 5120
CU0, CS0, TA0 = 2048, 6144, 7168


def await_count(eng, sem, count):
    if not (isinstance(count, int) and count == 0):
        eng.wait_ge(sem, count)


class Chain:

    def __init__(self, eng, sem):
        self.eng, self.sem, self.base, self.inside, self.turn = eng, sem, 0, 0, None

    def link(self, ins):
        self.inside += 1
        ins.then_inc(self.sem, 1)
        at = self.base + self.inside
        if self.turn is not None:
            i, first, per = self.turn
            at = (i - first) * per + at if first else i * per + at
        self.eng.wait_ge(self.sem, at)

    @contextmanager
    def loop(self, first, end, per):
        self.base, self.inside = self.base + self.inside, 0
        with self.eng.Fori(first, end) as i:
            self.turn = (i, first, per)
            yield i
        assert self.inside == per, (self.inside, per)
        self.base, self.inside, self.turn = self.base + per * (end - first), 0, None


def hybrid_layer(nc, x, mem, w8, wup, wmem, wout, g_pre, g_mem, g_post, w_conv, sink,
                 cos, sin, mask, ident_in, out):
    ctx = ExitStack()
    with ctx:
        def sb(name, shape, dt=F32):
            return ctx.enter_context(nc.sbuf_tensor(name, shape, dt))

        def psum(name, shape):
            return ctx.enter_context(nc.psum_tensor(name, shape, F32))

        def sem(name):
            return ctx.enter_context(nc.semaphore(name))

        h_hi = sb("h_hi", [P, KC, SEQ], F32R)
        h_lo = sb("h_lo", [P, KC, SEQ], F32R)
        y_hi = sb("y_hi", [P, AC, SEQ], F32R)
        y_lo = sb("y_lo", [P, AC, SEQ], F32R)
        area_m = sb("area_m", [P, KC * SEQ])
        raw = sb("raw", [P, 2, D])
        w_hi = sb("w_hi", [P, 2, D], F32R)
        w_lo = sb("w_lo", [P, 2, D], F32R)
        with nc.sbuf_tensor("area_a", [P, AREA_A], F32) as area_a:
            pass
        area_r = sb("area_r", [P, AREA_A], F32R)
        maskb = sb("maskb", [P, 5 * P])
        ident = sb("ident", [P, P])
        gpre = sb("gpre", [P, KC])
        gmem = sb("gmem", [P, KC])
        wconv = sb("wconv", [P, 3, AC])
        sinkb = sb("sinkb", [P, HEADS])
        st = sb("st", [P, 12, 8])

        merged = area_m[:, :].rearrange("p (k s) -> p k s", k=KC)
        qT = area_a[:, Q0:K0].rearrange("p (c s) -> p c s", c=AC)
        kT = area_a[:, K0:K0 + SEQ]
        vtok = area_a[:, V0:V0 + SEQ].rearrange("p (b d) -> p b d", b=NB)
        qz = area_a[:, QZ0:QZ0 + 2 * GROUP * P].rearrange("p (g h q) -> p g h q", g=2, h=GROUP)
        probs = area_a[:, P0:P0 + GROUP * WIN].rearrange("p (h k) -> p h k", h=GROUP)
        probsT = area_a[:, PT0:PT0 + 3 * GROUP * P].rearrange("p (j h q) -> p j h q", j=3, h=GROUP)
        vwin = area_a[:, VW0:VW0 + 3 * 2 * P].rearrange("p (j g d) -> p j g d", j=3, g=2)
        sig = area_a[:, SIG0:SIG0 + SEQ]
        conv_c = area_m[:, CS0:CS0 + SEQ]
        conv_cu = area_m[:, CU0:CU0 + SEQ + 2]
        conv_t = area_m[:, TA0:TA0 + SEQ]
        q_raw = area_m[:, QRAW0:QRAW0 + SEQ]
        q_swap = area_m[:, SWAP0:SWAP0 + SEQ]
        cosb = area_m[:, COS0:COS0 + SEQ]
        sinb = area_m[:, SIN0:SIN0 + SEQ]
        rot_t = area_m[:, ROT0:ROT0 + SEQ]
        vT = area_m[:, VT0:VT0 + SEQ]
        mkT = area_a[:, MK0:MK0 + MHEADS * MEM].rearrange("p (h m) -> p h m", h=MHEADS)
        mv = area_a[:, MV0:MV0 + 2 * AW].rearrange("p (b d) -> p b d", b=2)
        memx = area_a[:, MX0:MX0 + 2 * D].rearrange("p (b d) -> p b d", b=2)
        mn_hi = area_r[:, MNH0:MNH0 + KC * MEM].rearrange("p (k m) -> p k m", k=KC)
        mn_lo = area_r[:, MNL0:MNL0 + KC * MEM].rearrange("p (k m) -> p k m", k=KC)
        mprobs = area_a[:, MP0:MP0 + MHEADS * MEM].rearrange("p (h m) -> p h m", h=MHEADS)
        mprobsT = area_a[:, MPT0:MPT0 + 2 * MHEADS * P].rearrange("p (b h q) -> p b h q", b=2, h=MHEADS)
        mqz = area_a[:, MQZ0:MQZ0 + MHEADS * P].rearrange("p (h q) -> p h q", h=MHEADS)
        wout_raw = area_a[:, 0:KC * D]
        gpostb = area_a[:, GP0:GP0 + D]
        tout = area_a[:, TO0:TO0 + 2 * D].rearrange("p (b d) -> p b d", b=2)
        wo_hi = h_hi[:, :, :].rearrange("p k s -> p (k s)")
        wo_lo = h_lo[:, :, :].rearrange("p k s -> p (k s)")
        mb_hi = w_hi[:, :, :].rearrange("p b d -> p (b d)")
        mb_lo = w_lo[:, :, :].rearrange("p b d -> p (b d)")

        pm = psum("pm", [P, 2, SEQ])
        sa = psum("sa", [P, 3, HALF])
        pv = psum("pv", [P, HALF])

        x_landed = [sem(f"x_landed{b}") for b in range(NB)]
        ident_landed = sem("ident_landed")
        small_landed = sem("small_landed")
        st_cleared = sem("st_cleared")
        rope_landed = sem("rope_landed")
        mem_landed = sem("mem_landed")
        gpost_landed = sem("gpost_landed")
        wout_landed = [sem(f"wout_landed{n}") for n in range(2)]
        raw_landed = [sem(f"raw_landed{p}") for p in range(2)]
        xres_landed = [sem(f"xres_landed{p}") for p in range(2)]
        stored = [sem(f"stored{p}") for p in range(2)]
        ssq_act = sem("ssq_act")
        var_made, root_made, xs_made = sem("var_made"), sem("root_made"), sem("xs_made")
        x_turned, h_hi_made, h_made = sem("x_turned"), sem("h_hi_made"), sem("h_made")
        hi_made, lo_made = sem("hi_made"), sem("lo_made")
        tile_done = sem("tile_done")
        up_half_done = sem("up_half_done")
        drained = [sem(f"drained{p}") for p in range(2)]
        swapped, roped = sem("swapped"), sem("roped")
        v_turned, v_made = sem("v_turned"), sem("v_made")
        sig_made, y_made, y_hi_made, y_ready = sem("sig_made"), sem("y_made"), sem("y_hi_made"), sem("y_ready")
        q_staged, v_staged = sem("q_staged"), sem("v_staged")
        scored, masked, nm_ready, exped = sem("scored"), sem("masked"), sem("nm_ready"), sem("exped")
        p_ready, turned, pt_act, pt_dve = sem("p_ready"), sem("turned"), sem("pt_act"), sem("pt_dve")
        pv_done, o_taken = sem("pv_done"), sem("o_taken")
        memx_ready, mem_turned, mn_made = sem("memx_ready"), sem("mem_turned"), sem("mn_made")
        mq_staged, mscored, mnm_ready, mexped = sem("mq_staged"), sem("mscored"), sem("mnm_ready"), sem("mexped")
        mp_ready, mturned, merged_done = sem("mp_ready"), sem("mturned"), sem("merged_done")
        wo_hi_made, wo_lo_made = sem("wo_hi_made"), sem("wo_lo_made")
        mb_hi_made, mb_lo_made = sem("mb_hi_made"), sem("mb_lo_made")
        sq_made, out_var, out_root, out_ready = sem("sq_made"), sem("out_var"), sem("out_root"), sem("out_ready")
        act_chain, dve_chain = sem("act_chain"), sem("dve_chain")

        block = ctx.enter_context(nc.Block())

        @block.sync
        def _(sp):
            for b in range(NB):
                sp.dma_start(area_m[:, b * D:(b + 1) * D], x[b * P:(b + 1) * P, :]).then_inc(x_landed[b], 16)
                if b == 1:
                    sp.dma_start(ident[:, :], ident_in).then_inc(ident_landed, 16)
                    sp.dma_start(gpre[:, :], g_pre).then_inc(ident_landed, 16)
                if b == 5:
                    sp.dma_start(raw[:, 0, :], w8[0]).then_inc(raw_landed[0], 16)
            sp.dma_start(raw[:, 1, :], w8[1]).then_inc(raw_landed[1], 16)
            for dst, src in ((gmem[:, :], g_mem), (wconv[:, :, :], w_conv), (sinkb[:, :], sink), (maskb[:, :], mask)):
                sp.dma_start(dst, src).then_inc(small_landed, 16)
            sp.wait_ge(x_turned, 8)
            sp.dma_start(cosb, cos).then_inc(rope_landed, 16)
            sp.dma_start(sinb, sin).then_inc(rope_landed, 16)

            with sp.Fori(1, T_MA // 2) as i:
                for p in range(2):
                    sp.wait_ge(lo_made, 2 * i + (p - 1))
                    sp.dma_start(raw[:, p, :], w8[2 * i + p]).then_inc(raw_landed[p], 16)

            def merge_loads(sp, i, t0, w8_0, up0):
                sp.wait_ge(lo_made, 2 * i + (t0 - 1))
                sp.dma_start(raw[:, 0, :], w8[i + w8_0]).then_inc(raw_landed[0], 16)
                sp.wait_ge(lo_made, 2 * i + t0)
                sp.dma_start(raw[:, 1, 0:AW], wup[i + up0]).then_inc(raw_landed[1], 16)

            with sp.Fori(0, KC) as i:
                merge_loads(sp, i, T_MA, T_MA, 0)
            n8 = T_MA + KC
            with sp.Fori(0, AC) as i:
                for p in range(2):
                    sp.wait_ge(lo_made, 2 * i + (T_ZB + p - 1))
                    sp.dma_start(raw[:, p, :], w8[2 * i + (n8 + p)]).then_inc(raw_landed[p], 16)
            n8 += 2 * AC
            sp.wait_ge(pv_done, 2 * NB)
            for b in range(2):
                sp.dma_start(memx[:, b, :], mem[b * P:(b + 1) * P, :]).then_inc(mem_landed, 16)
            with sp.Fori(0, MHEADS) as i:
                for p in range(2):
                    sp.wait_ge(lo_made, 2 * i + (T_MEM + p - 1))
                    sp.dma_start(raw[:, p, :], wmem[2 * i + p]).then_inc(raw_landed[p], 16)
            with sp.Fori(0, KC) as i:
                merge_loads(sp, i, T_MB, n8, KC)
            n8 += KC
            with sp.Fori(0, AC // 2) as i:
                for p in range(2):
                    sp.wait_ge(lo_made, 2 * i + (T_ZM + p - 1))
                    sp.dma_start(raw[:, p, :], w8[2 * i + (n8 + p)]).then_inc(raw_landed[p], 16)
            n8 += AC
            with sp.Fori(0, KC) as i:
                merge_loads(sp, i, T_MM, n8, 2 * KC)
            sp.wait_ge(y_ready, 3 * AC)
            for n in range(2):
                sp.dma_start(wout_raw[:, n * KC * HALF:(n + 1) * KC * HALF], wout[n]).then_inc(wout_landed[n], 16)
            sp.dma_start(gpostb, g_post).then_inc(gpost_landed, 16)
            sp.wait_ge(lo_made, T_OUT)
            for p in range(2):
                sp.dma_start(raw[:, p, :], x[p * P:(p + 1) * P, :]).then_inc(xres_landed[p], 16)
            with sp.Fori(0, NB // 2 - 1) as i:
                for p in range(2):
                    sp.wait_ge(out_ready, 2 * i + (p + 1))
                    sp.dma_start(out[bass.ds((2 * i + p) * P, P), :], tout[:, p, :]).then_inc(stored[p], 16)
                    sp.dma_start(raw[:, p, :], x[bass.ds((2 * i + (p + 2)) * P, P), :]).then_inc(xres_landed[p], 16)
            for b in range(NB - 2, NB):
                sp.wait_ge(out_ready, b + 1)
                sp.dma_start(out[b * P:(b + 1) * P, :], tout[:, b % 2, :]).then_inc(stored[b % 2], 16)
            for p in range(2):
                sp.wait_ge(stored[p], 16 * (NB // 2))

        @block.gpsimd
        def _(pool):
            def low_part(p, nth, width=D):
                pool.wait_ge(hi_made, nth)
                nc.gpsimd.tensor_tensor(w_lo[:, p, 0:width], raw[:, p, 0:width], w_hi[:, p, 0:width].bitcast(F32),
                                        ALU.subtract).then_inc(lo_made, 1)

            low_part(0, 1)
            pool.wait_ge(x_turned, 8)
            nc.gpsimd.memset(q_swap, 0.0).then_inc(rope_landed, 16)
            low_part(1, 2)
            for t0, end, width in ((2, T_MA, D), (T_MA, T_ZB, AW), (T_ZB, T_MEM, D),
                                   (T_MB + 2, T_ZM, AW), (T_ZM, T_MM, D), (T_MM, T_OUT, AW)):
                if t0 == T_MB + 2:
                    pool.wait_ge(lo_made, t0)
                with pool.Fori(t0 // 2, end // 2) as i:
                    low_part(0, 2 * i + 1)
                    low_part(1, 2 * i + 2, width)

        @block.tensor
        def _(pe):
            def product(t_half, p, chunks, src_hi, src_lo, nth, first=0, last=None, ready=None):
                last = 2 * chunks if last is None else last
                if first == 0:
                    await_count(pe, drained[p], t_half)
                for step in range(first, last):
                    half, k = divmod(step, chunks)
                    if ready is not None:
                        ready(step)
                    if step == 0:
                        pe.wait_ge(hi_made, nth)
                        pe.wait_ge(lo_made, nth)
                    cols = slice(half * HALF, (half + 1) * HALF)
                    hi, lo = w_hi[:, p, k * P:(k + 1) * P], w_lo[:, p, k * P:(k + 1) * P]
                    pe.matmul(pm[:, p, cols], hi, src_hi[:, k, cols], start=(k == 0), stop=False)
                    pe.matmul(pm[:, p, cols], hi, src_lo[:, k, cols], start=False, stop=False)
                    mm = pe.matmul(pm[:, p, cols], lo, src_hi[:, k, cols], start=False, stop=(k == chunks - 1))
                    if step == 2 * chunks - 1:
                        mm.then_inc(tile_done, 1)
                    elif k == chunks - 1 and chunks == AC:
                        mm.then_inc(up_half_done, 1)

            def from_h(i, t0, q=0, first=0, last=None, ready=None):
                product((t0 + q) // 2 + i, q % 2, KC, h_hi, h_lo, 2 * i + (t0 + q + 1),
                        first, last, ready)

            def from_y(i, t0, first=0, last=None):
                product(t0 // 2 + i, 1, AC, y_hi, y_lo, 2 * i + (t0 + 2), first, last)

            spare = [sa[:, 0, :], sa[:, 1, :], sa[:, 2, :], pv[:, :]]

            def turn_x(n):
                half, k = divmod(n, KC)
                if k == 0:
                    pe.wait_ge(xs_made, 2 * half + 2)
                if n >= 4:
                    pe.wait_ge(h_made, n - 3)
                for b in range(4):
                    src = area_m[:, (4 * half + b) * D + k * P:(4 * half + b) * D + (k + 1) * P]
                    mm = pe.transpose(spare[n % 4][:, b * P:(b + 1) * P], src, ident[:, :])
                mm.then_inc(x_turned, 1)

            def turn_then_wait(step):
                if step % KC == 0:
                    for n in range(step, step + 4):
                        turn_x(n)
                elif step % KC <= 4:
                    turn_x(step + 3)
                pe.wait_ge(h_made, step + 1)

            pe.wait_ge(ident_landed, 32)
            for q in range(2 + AC):
                p = q % 2
                from_h(0, T_QKV, q, ready=turn_then_wait if q == 0 else None)
                if q == 2:
                    pe.wait_ge(drained[1], 1)
                    for n in range(2):
                        for b in range(4):
                            mm = pe.transpose(sa[:, n, b * P:(b + 1) * P],
                                              vT[:, (4 * n + b) * P:(4 * n + b + 1) * P], ident[:, :])
                        mm.then_inc(v_turned, 1)

            def conv_tile(j, q):
                product(2 * j + (T_CONV + q) // 2, q % 2, KC, h_hi, h_lo, 4 * j + (T_CONV + q + 1))

            with pe.Fori(0, AC - 1) as j:
                for q in range(4):
                    conv_tile(j, q)

            def scores(i, g, window):
                if g == 0:
                    pe.wait_ge(q_staged, i + 1)
                for h in range(GROUP):
                    b = h % 2
                    if h < 2:
                        await_count(pe, pt_dve, 2 * i + g)
                        await_count(pe, pt_act, 4 * i + 2 * g)
                        pe.wait_ge(v_made, 2)
                    else:
                        pe.wait_ge(masked, 8 * i + (4 * g + h - 1))
                    pe.matmul(sa[:, b, 0:WIN], qz[:, g, h, :], window, start=True, stop=True).then_inc(scored, 1)

            def turn_probs(i, g):
                pe.wait_ge(p_ready, 2 * i + (g + 1))
                for j, bank in enumerate((2, 0, 1)):
                    for h in range(GROUP):
                        mm = pe.transpose(sa[:, bank, h * P:(h + 1) * P], probs[:, h, j * P:(j + 1) * P], ident[:, :])
                    mm.then_inc(turned, 1)

            def values(i, g):
                if g == 0:
                    pe.wait_ge(v_staged, i + 1)
                    await_count(pe, o_taken, i)
                for j in range(3):
                    if j == 1:
                        pe.wait_ge(pt_dve, 2 * i + (g + 1))
                    else:
                        pe.wait_ge(pt_act, 4 * i + (2 * g + 1 + j // 2))
                    mm = pe.matmul(pv[:, :], vwin[:, j, g, :], probsT[:, j, :, :].rearrange("p h q -> p (h q)"),
                                   start=(g == 0 and j == 0), stop=(g == 1 and j == 2))
                mm.then_inc(pv_done, 1)

            def merge_a(i, window, first=False):
                if not first:
                    scores(i, 0, window)
                    values(i - 1, 1)
                from_h(i, T_MA, 0, 0, 10)
                turn_probs(i, 0)
                from_h(i, T_MA, 0, 10, 12)
                scores(i, 1, window)
                values(i, 0)
                from_h(i, T_MA, 0, 12)
                if first:
                    pe.wait_ge(y_ready, AC)
                from_y(i, T_MA, 0, 6)
                turn_probs(i, 1)
                from_y(i, T_MA, 6)

            for q in range(3):
                conv_tile(AC - 1, q)
            scores(0, 0, kT[:, 0:WIN])
            conv_tile(AC - 1, 3)
            merge_a(0, kT[:, 0:WIN], first=True)
            with pe.Fori(1, NB - 1) as i:
                merge_a(i, kT[:, bass.ds((i - 1) * P, WIN)])
            merge_a(NB - 1, kT[:, SEQ - WIN:SEQ])
            values(NB - 1, 1)

            with pe.Fori(0, AC // 2) as i:
                for q in range(2):
                    from_h(i, T_ZB, q)
            for q in range(AC):
                from_h(0, T_MQ, q)
                if q == 1:
                    pe.wait_ge(memx_ready, 1)
                    for n in range(4):
                        for kk in range(2):
                            for b in range(2):
                                k = 2 * n + kk
                                mm = pe.transpose(spare[n][:, kk * MEM + b * P:kk * MEM + (b + 1) * P],
                                                  memx[:, b, k * P:(k + 1) * P], ident[:, :])
                        mm.then_inc(mem_turned, 1)

            pe.wait_ge(mn_made, 4)
            parts = ((w_hi, mn_hi), (w_hi, mn_lo), (w_lo, mn_hi))
            for n in range(MHEADS):
                p, t = n % 2, T_MEM + n
                pe.wait_ge(drained[p], t // 2)
                pe.wait_ge(hi_made, t + 1)
                for which, (w, m) in enumerate(parts):
                    if which == 2:
                        pe.wait_ge(lo_made, t + 1)
                    for k in range(KC):
                        mm = pe.matmul(pm[:, p, 0:MEM], w[:, p, k * P:(k + 1) * P], m[:, k, :],
                                       start=(which == 0 and k == 0), stop=(which == 2 and k == KC - 1))
                mm.then_inc(tile_done, 1)
            pe.wait_ge(drained[1], (T_MEM + MHEADS) // 2)
            for n in range(MHEADS):
                p, t = n % 2, T_MEM + MHEADS + n
                pe.wait_ge(hi_made, t + 1)
                for which, (w, m) in enumerate(parts):
                    if which == 2:
                        pe.wait_ge(lo_made, t + 1)
                    for kk in range(2):
                        for b in range(2):
                            mm = pe.matmul(pm[:, 1, b * HALF:(b + 1) * HALF], m[:, 2 * n + kk, b * P:(b + 1) * P],
                                           w[:, p, kk * AW:(kk + 1) * AW],
                                           start=(n == 0 and which == 0 and kk == 0),
                                           stop=(n == MHEADS - 1 and which == 2 and kk == 1))
                            if n < MHEADS - 1 and which == 0 and kk == 0 and b == 0:
                                mm.then_inc(drained[p], 1)
                mm.then_inc(tile_done, 1)

            with pe.Fori(0, KC) as i:
                from_h(i, T_MB, 0, 0, 3)
                pe.wait_ge(mq_staged, i + 1)
                pe.wait_ge(drained[1], (T_MEM + 8) // 2)
                for b in range(2):
                    pe.wait_ge(*((pt_act, i + 4 * NB), (pt_dve, i + 2 * NB))[b])
                    for h in range(2 * b, 2 * b + 2):
                        mm = pe.matmul(sa[:, b, (h % 2) * MEM:(h % 2 + 1) * MEM], mqz[:, h, :], mkT[:, h, :],
                                       start=True, stop=True)
                    mm.then_inc(mscored, 1)
                from_h(i, T_MB, 0, 3)
                pe.wait_ge(mp_ready, i + 1)
                for b in range(2):
                    for h in range(MHEADS):
                        mm = pe.transpose(sa[:, b, h * P:(h + 1) * P], mprobs[:, h, b * P:(b + 1) * P], ident[:, :])
                    mm.then_inc(mturned, 1)
                pe.wait_ge(y_ready, 2 * AC)
                from_y(i, T_MB, 0, 6)
                pe.wait_ge(pt_act, i + (4 * NB + 1))
                pe.wait_ge(pt_dve, i + (2 * NB + 1))
                pe.wait_ge(o_taken, i + NB)
                for h in range(MHEADS):
                    for b in range(2):
                        mm = pe.matmul(pv[:, h * P:(h + 1) * P], mv[:, b, h * P:(h + 1) * P], mprobsT[:, b, h, :],
                                       start=(b == 0), stop=(b == 1))
                mm.then_inc(pv_done, 1)
                from_y(i, T_MB, 6)

            with pe.Fori(0, AC // 2) as i:
                for q in range(2):
                    from_h(i, T_ZM, q)
            with pe.Fori(0, KC) as i:
                from_h(i, T_MM)
                pe.wait_ge(y_ready, 3 * AC)
                from_y(i, T_MM)

            def out_block(i, p, first=False):
                b_no = 2 * i + p
                pe.wait_ge(drained[p], T_OUT // 2 + i)
                pe.wait_ge(mb_hi_made, b_no + 1)
                pe.wait_ge(mb_lo_made, b_no + 1)
                for half in range(2):
                    for k in range(KC):
                        if first:
                            pe.wait_ge(wo_lo_made, half * KC + k + 1)
                        n = half * KC + k
                        hi = mb_hi[:, (p * KC + k) * P:(p * KC + k + 1) * P]
                        lo = mb_lo[:, (p * KC + k) * P:(p * KC + k + 1) * P]
                        dst = pm[:, p, half * HALF:(half + 1) * HALF]
                        pe.matmul(dst, hi, wo_hi[:, n * HALF:(n + 1) * HALF], start=(k == 0), stop=False)
                        pe.matmul(dst, lo, wo_hi[:, n * HALF:(n + 1) * HALF], start=False, stop=False)
                        mm = pe.matmul(dst, hi, wo_lo[:, n * HALF:(n + 1) * HALF], start=False, stop=(k == KC - 1))
                mm.then_inc(tile_done, 1)

            out_block(0, 0, first=True)
            out_block(0, 1)
            with pe.Fori(1, NB // 2) as i:
                for p in range(2):
                    out_block(i, p)

        @block.scalar
        def _(act):
            def split_next(p, t_half, nth):
                act.wait_ge(raw_landed[p], 16 * t_half + 16)
                nc.scalar.activation(w_hi[:, p, :], raw[:, p, :], ACT.Copy).then_inc(hi_made, 1)

            def after_tile(t0, per, i, p):
                act.wait_ge(tile_done, per * i + (t0 + 1))
                split_next(p, (per // 2) * i + (t0 + 2) // 2, per * i + (t0 + 3))

            act.wait_ge(st_cleared, 1)
            nc.scalar.activation(st[:, 11, 0:1], st[:, 10, 0:1], ACT.Sqrt)

            def high_of_h(n):
                half, k = divmod(n, KC)
                bank = [sa[:, 0, :], sa[:, 1, :], sa[:, 2, :], pv[:, :]][n % 4]
                act.wait_ge(x_turned, n + 1)
                nc.scalar.activation(h_hi[:, k, half * HALF:(half + 1) * HALF], bank, ACT.Identity,
                                     scale=gpre[:, k:k + 1]).then_inc(h_hi_made, 1)

            def square_sum(b):
                act.wait_ge(x_landed[b], 16)
                nc.scalar.activation(area_a[:, b * D:(b + 1) * D], area_m[:, b * D:(b + 1) * D],
                                     ACT.Square, accum_out=st[:, 0, b:b + 1]).then_inc(ssq_act, 1)

            def roots(pair):
                cols = slice(2 * pair, 2 * pair + 2)
                act.wait_ge(var_made, pair + 1)
                nc.scalar.activation(st[:, 2, cols], st[:, 1, cols], ACT.Sqrt).then_inc(root_made, 1)

            for b in range(5):
                square_sum(b)
                if b in (1, 3):
                    roots(b // 2)
            act.wait_ge(ident_landed, 32)
            high_of_h(0)
            square_sum(5)
            for n in (1, 2):
                high_of_h(n)
            roots(2)
            split_next(0, 0, 1)
            for n in range(3, KC):
                high_of_h(n)
            for b in (6, 7):
                square_sum(b)
            roots(3)
            split_next(1, 0, 2)
            for n in range(KC, 2 * KC):
                high_of_h(n)

            act.wait_ge(h_made, 2 * KC)
            for q in range(2 + AC):
                p = q % 2
                act.wait_ge(tile_done, q + 1)
                if q == 1:
                    nc.scalar.copy(vT, pm[:, 1, :]).then_inc(drained[1], 1)
                else:
                    n = q if q == 0 else q - 1
                    if n:
                        act.wait_ge(roped, n)
                    else:
                        act.wait_ge(rope_landed, 48)
                    nc.scalar.copy(q_raw, pm[:, p, :]).then_inc(drained[p], 1)
                    act.wait_ge(drained[p], q // 2 + 1)
                    for row in (0, HEAD):
                        half_rot = ROT // 2
                        act.dma_start(q_swap[row:row + half_rot, :],
                                      q_raw[row + half_rot:row + ROT, :]).then_inc(swapped, 16)
                        act.dma_start(q_swap[row + half_rot:row + ROT, :],
                                      q_raw[row:row + half_rot, :]).then_inc(swapped, 16)
                split_next(p, (q + 2) // 2, q + 3)
                if q == 2:
                    for n in range(2):
                        act.wait_ge(v_turned, n + 1)
                        nc.scalar.copy(vtok[:, 4 * n:4 * n + 4, :],
                                       sa[:, n, :].rearrange("p (b d) -> p b d", b=4)).then_inc(v_made, 1)

            def conv_tiles(j):
                act.wait_ge(tile_done, 4 * j + (T_CONV + 1))
                act.wait_ge(drained[1], 2 * j + T_CONV // 2)
                nc.scalar.copy(conv_c, pm[:, 0, :]).then_inc(drained[0], 1)
                split_next(0, 2 * j + (T_CONV + 2) // 2, 4 * j + (T_CONV + 3))
                after_tile(T_CONV + 1, 4, j, 1)
                after_tile(T_CONV + 2, 4, j, 0)

            def conv_z(j):
                act.wait_ge(tile_done, 4 * j + (T_CONV + 4))
                act.wait_ge(drained[1], 2 * j + (T_CONV // 2 + 1))
                nc.scalar.activation(sig, pm[:, 1, :], ACT.Sigmoid).then_inc(sig_made, 1)
                split_next(1, 2 * j + (T_CONV + 5) // 2, 4 * j + (T_CONV + 6))
                act.wait_ge(y_made, j + 1)
                nc.scalar.activation(y_hi[:, j, :], sig, ACT.Copy).then_inc(y_hi_made, 1)

            with act.Fori(0, AC - 1) as j:
                conv_tiles(j)
                conv_z(j)

            def exps(i, g):
                act.wait_ge(nm_ready, 2 * i + (g + 1))
                nc.scalar.activation(st[:, 4, 4:8], st[:, 4, 0:4], ACT.Exp)
                for h in range(GROUP):
                    ins = nc.scalar.activation(probs[:, h, :], probs[:, h, :], ACT.Exp,
                                               bias=st[:, 3, h:h + 1], accum_out=st[:, 5, h:h + 1])
                ins.then_inc(exped, 1)

            def take_probs(i, g):
                await_count(act, pv_done, 2 * i + g)
                for n, (j, bank) in enumerate(((0, 2), (2, 1))):
                    act.wait_ge(turned, 6 * i + (3 * g + j + 1))
                    nc.scalar.copy(probsT[:, j, :, :],
                                   sa[:, bank, :].rearrange("p (h q) -> p h q", h=GROUP)).then_inc(pt_act, 1)

            def merge_a(i):
                take_probs(i, 0)
                exps(i, 1)
                act.wait_ge(tile_done, 2 * i + (T_MA + 1))
                act.wait_ge(drained[1], i + T_MA // 2)
                nc.scalar.activation(sig, pm[:, 0, :], ACT.Sigmoid).then_inc(drained[0], 1)
                split_next(0, i + (T_MA + 2) // 2, 2 * i + (T_MA + 3))
                take_probs(i, 1)
                act.wait_ge(tile_done, 2 * i + (T_MA + 2))
                split_next(1, i + (T_MA + 2) // 2, 2 * i + (T_MA + 4))

            conv_tiles(AC - 1)
            exps(0, 0)
            conv_z(AC - 1)
            act.wait_ge(y_ready, AC)
            merge_a(0)
            with act.Fori(1, NB) as i:
                exps(i, 0)
                merge_a(i)

            def gated(i, q, t0, n0):
                p = q
                act.wait_ge(tile_done, 2 * i + (t0 + q + 1))
                act.wait_ge(y_ready, 2 * i + (n0 + q))
                nc.scalar.activation(sig, pm[:, p, :], ACT.Sigmoid).then_inc(sig_made, 1)
                split_next(p, i + (t0 + q + 2) // 2, 2 * i + (t0 + q + 3))
                act.wait_ge(y_made, 2 * i + (n0 + q + 1))
                nc.scalar.activation(y_hi[:, 2 * i + q, :], sig, ACT.Copy).then_inc(y_hi_made, 1)

            act.wait_ge(drained[1], T_ZB // 2)
            with act.Fori(0, AC // 2) as i:
                for q in range(2):
                    gated(i, q, T_ZB, AC)
            act.wait_ge(var_made, 5)
            nc.scalar.activation(st[:, 2, 0:2], st[:, 1, 0:2], ACT.Sqrt).then_inc(root_made, 1)
            for q in range(AC):
                after_tile(T_MQ + q, 2, 0, q % 2)
            for n in range(2 * MHEADS):
                p, t = n % 2, T_MEM + n
                act.wait_ge(tile_done, t + 1)
                if n < MHEADS:
                    nc.scalar.copy(mkT[:, n, :], pm[:, p, 0:MEM]).then_inc(drained[p], 1)
                elif n == 2 * MHEADS - 1:
                    nc.scalar.copy(mv, pm[:, 1, :].rearrange("p (b d) -> p b d", b=2)).then_inc(drained[1], 1)
                split_next(p, (t + 2) // 2, t + 3)

            act.wait_ge(y_ready, 2 * AC)
            with act.Fori(0, KC) as i:
                act.wait_ge(mnm_ready, i + 1)
                for h in range(MHEADS):
                    ins = nc.scalar.activation(mprobs[:, h, :], sa[:, h // 2, (h % 2) * MEM:(h % 2 + 1) * MEM],
                                               ACT.Exp, bias=st[:, 3, h:h + 1], scale=float(P) ** -0.5,
                                               accum_out=st[:, 5, h:h + 1])
                ins.then_inc(mexped, 1)
                act.wait_ge(tile_done, 2 * i + (T_MB + 1))
                nc.scalar.activation(sig, pm[:, 0, :], ACT.Sigmoid).then_inc(drained[0], 1)
                split_next(0, i + (T_MB + 2) // 2, 2 * i + (T_MB + 3))
                act.wait_ge(mturned, 2 * i + 1)
                act.wait_ge(pv_done, i + 2 * NB)
                nc.scalar.copy(mprobsT[:, 0, :, :],
                               sa[:, 0, :].rearrange("p (h q) -> p h q", h=MHEADS)).then_inc(pt_act, 1)
                act.wait_ge(tile_done, 2 * i + (T_MB + 2))
                split_next(1, i + (T_MB + 2) // 2, 2 * i + (T_MB + 4))

            act.wait_ge(merged_done, KC)
            with act.Fori(0, AC // 2) as i:
                for q in range(2):
                    gated(i, q, T_ZM, 2 * AC)

            def gate_m(i, more):
                act.wait_ge(tile_done, 2 * i + (T_MM + 1))
                act.wait_ge(merged_done, i + KC)
                nc.scalar.activation(sig, pm[:, 0, :], ACT.Sigmoid).then_inc(drained[0], 1)
                if more:
                    split_next(0, i + (T_MM + 2) // 2, 2 * i + (T_MM + 3))
                    act.wait_ge(tile_done, 2 * i + (T_MM + 2))
                    split_next(1, i + (T_MM + 2) // 2, 2 * i + (T_MM + 4))

            act.wait_ge(y_ready, 3 * AC)
            with act.Fori(0, KC - 1) as i:
                gate_m(i, True)
            gate_m(KC - 1, False)

            def wout_high(half):
                act.wait_ge(wout_landed[half], 16)
                for k in range(KC):
                    n = half * KC + k
                    nc.scalar.activation(wo_hi[:, n * HALF:(n + 1) * HALF], wout_raw[:, n * HALF:(n + 1) * HALF],
                                         ACT.Copy).then_inc(wo_hi_made, 1)

            def merged_high(p, at):
                nc.scalar.activation(mb_hi[:, p * D:(p + 1) * D].rearrange("p (k q) -> p k q", k=KC), at,
                                     ACT.Copy).then_inc(mb_hi_made, 1)

            wout_high(0)
            act.wait_ge(merged_done, 2 * KC)
            merged_high(0, merged[:, :, 0:P])
            wout_high(1)
            act.wait_ge(tile_done, T_OUT)
            merged_high(1, merged[:, :, P:2 * P])

            def out_block(i, p, more):
                act.wait_ge(tile_done, 2 * i + (T_OUT + p + 1))
                await_count(act, stored[p], 16 * i)
                nc.scalar.activation(tout[:, p, :], pm[:, p, :], ACT.Square,
                                     accum_out=st[:, 6, p:p + 1]).then_inc(sq_made, 1)
                if more:
                    merged_high(p, merged[:, :, bass.ds((2 * i + (p + 2)) * P, P)])
                act.wait_ge(out_var, 2 * i + (p + 1))
                nc.scalar.activation(st[:, 8, p:p + 1], st[:, 7, p:p + 1], ACT.Sqrt).then_inc(out_root, 1)

            for p in range(2):
                out_block(0, p, True)
            with act.Fori(1, NB // 2 - 1) as i:
                for p in range(2):
                    out_block(i, p, True)
            for p in range(2):
                out_block(NB // 2 - 1, p, False)

        @block.vector
        def _(dve):
            chain = Chain(dve, dve_chain)
            link = chain.link

            def inv_root(var, root, r, t):
                link(nc.vector.reciprocal(r, root))
                link(nc.vector.tensor_tensor(t, r, r, ALU.mult))
                link(nc.vector.tensor_tensor(t, t, var, ALU.mult))
                link(nc.vector.tensor_scalar(t, t, -0.5, 1.5, ALU.mult, ALU.add))
                link(nc.vector.tensor_tensor(r, r, t, ALU.mult))

            nc.vector.memset(st[:, :, :], 0.0).then_inc(st_cleared, 1)
            dve.wait_ge(st_cleared, 1)

            def scale_pair(pair):
                cols = slice(2 * pair, 2 * pair + 2)
                dve.wait_ge(ssq_act, 2 * pair + 2)
                nc.vector.tensor_scalar(st[:, 1, cols], st[:, 0, cols], 1.0 / D, EPS, ALU.mult,
                                        ALU.add).then_inc(var_made, 1)
                dve.wait_ge(var_made, pair + 1)
                dve.wait_ge(root_made, pair + 1)
                inv_root(st[:, 1, cols], st[:, 2, cols], st[:, 9, cols], st[:, 10, cols])
                for b in range(2 * pair, 2 * pair + 2):
                    ins = nc.vector.tensor_scalar(area_m[:, b * D:(b + 1) * D], area_m[:, b * D:(b + 1) * D],
                                                  st[:, 9, b:b + 1], None, ALU.mult)
                ins.then_inc(xs_made, 1)

            scale_pair(0)
            scale_pair(1)
            dve.wait_ge(ident_landed, 32)
            for n in range(2 * KC):
                half, k = divmod(n, KC)
                cols = slice(half * HALF, (half + 1) * HALF)
                bank = [sa[:, 0, :], sa[:, 1, :], sa[:, 2, :], pv[:, :]][n % 4]
                if n == 3:
                    scale_pair(2)
                if n == KC:
                    scale_pair(3)
                dve.wait_ge(h_hi_made, n + 1)
                nc.vector.scalar_tensor_tensor(out=h_lo[:, k, cols], in0=bank, scalar=gpre[:, k:k + 1],
                                               in1=h_hi[:, k, cols].bitcast(F32), op0=ALU.mult,
                                               op1=ALU.subtract).then_inc(h_made, 1)

            dve.wait_ge(rope_landed, 48)
            for n in range(1 + AC):
                dst = kT if n == 0 else qT[:, n - 1, :]
                dve.wait_ge(drained[0 if n == 0 else (n + 1) % 2], 1 if n == 0 else (n + 1) // 2 + 1)
                link(nc.vector.tensor_tensor(dst, q_raw, cosb, ALU.mult))
                dve.wait_ge(swapped, 64 * (n + 1))
                link(nc.vector.tensor_tensor(rot_t, q_swap, sinb, ALU.mult))
                nc.vector.tensor_tensor(dst, dst, rot_t, ALU.add).then_inc(roped, 1)

            dve.wait_ge(small_landed, 64)
            nc.vector.memset(conv_cu[:, 0:1], 0.0)
            link(nc.vector.memset(conv_cu[:, SEQ + 1:SEQ + 2], 0.0))

            def tap_weight(j, tap):
                return wconv[:, tap, j:j + 1] if isinstance(j, int) else wconv[:, tap, bass.ds(j, 1)]

            def conv_tiles(j):
                dve.wait_ge(tile_done, 4 * j + (T_CONV + 2))
                dve.wait_ge(drained[0], 2 * j + (T_CONV // 2 + 1))
                nc.vector.tensor_tensor(conv_cu[:, 1:SEQ + 1], pm[:, 1, :], conv_c, ALU.mult).then_inc(drained[1], 1)
                dve.wait_ge(drained[1], 2 * j + (T_CONV // 2 + 1))
                link(nc.vector.tensor_scalar(conv_t, conv_cu[:, 0:SEQ], tap_weight(j, 0), None, ALU.mult))
                for tap in (1, 2):
                    link(nc.vector.scalar_tensor_tensor(out=conv_t, in0=conv_cu[:, tap:tap + SEQ],
                                                        scalar=tap_weight(j, tap), in1=conv_t,
                                                        op0=ALU.mult, op1=ALU.add))
                dve.wait_ge(tile_done, 4 * j + (T_CONV + 3))
                nc.vector.tensor_tensor(conv_t, pm[:, 0, :], conv_t, ALU.mult).then_inc(drained[0], 1)

            def conv_z(j):
                dve.wait_ge(sig_made, j + 1)
                dve.wait_ge(drained[0], 2 * j + (T_CONV // 2 + 2))
                nc.vector.tensor_tensor(sig, pm[:, 1, :], sig, ALU.mult).then_inc(drained[1], 1)
                dve.wait_ge(drained[1], 2 * j + (T_CONV // 2 + 2))
                nc.vector.tensor_tensor(sig, conv_t, sig, ALU.mult).then_inc(y_made, 1)
                dve.wait_ge(y_hi_made, j + 1)
                nc.vector.tensor_tensor(y_lo[:, j, :], sig, y_hi[:, j, :].bitcast(F32),
                                        ALU.subtract).then_inc(y_ready, 1)
                dve.wait_ge(y_ready, j + 1)

            with chain.loop(0, AC - 1, 3) as j:
                conv_tiles(j)
                conv_z(j)

            nc.vector.memset(qz[HEAD:P, 0, :, :], 0.0)
            nc.vector.memset(qz[0:HEAD, 1, :, :], 0.0)
            nc.vector.memset(vwin[:, :, 0, HEAD:P], 0.0)
            link(nc.vector.memset(vwin[:, :, 1, 0:HEAD], 0.0))

            def stage_q(at):
                link(nc.vector.tensor_copy(qz[0:HEAD, 0, :, :], qT[0:HEAD, :, at]))
                nc.vector.tensor_copy(qz[HEAD:P, 1, :, :], qT[HEAD:P, :, at]).then_inc(q_staged, 1)

            def softmax_head(i, g, mask_at):
                for h in range(GROUP):
                    dve.wait_ge(scored, 8 * i + (4 * g + h + 1))
                    nc.vector.memset(st[:, 11, GROUP * g + h:GROUP * g + h + 1], 0.0)
                    nc.vector.tensor_tensor_reduce(
                        out=probs[:, h, :], in0=sa[:, h % 2, 0:WIN], in1=maskb[:, mask_at:mask_at + WIN],
                        scale=float(HEAD) ** -0.5, scalar=-3.0e38, op0=ALU.add, op1=ALU.max,
                        accum_out=st[:, 0, h:h + 1]).then_inc(masked, 1)
                dve.wait_ge(masked, 8 * i + (4 * g + 4))
                sinks = sinkb[:, GROUP * g:GROUP * g + GROUP]
                link(nc.vector.tensor_tensor(st[:, 1, 0:4], st[:, 0, 0:4], sinks, ALU.max))
                link(nc.vector.tensor_scalar(st[:, 3, 0:4], st[:, 1, 0:4], -1.0, None, ALU.mult))
                nc.vector.tensor_tensor(st[:, 4, 0:4], sinks, st[:, 3, 0:4], ALU.add).then_inc(nm_ready, 1)

            def softmax_tail(i, g):
                dve.wait_ge(exped, 2 * i + (g + 1))
                link(nc.vector.tensor_tensor(st[:, 5, 4:8], st[:, 5, 0:4], st[:, 4, 4:8], ALU.add))
                link(nc.vector.reciprocal(st[:, 6, 0:4], st[:, 5, 4:8]))
                for h in range(GROUP):
                    ins = nc.vector.tensor_scalar(probs[:, h, :], probs[:, h, :], st[:, 6, h:h + 1], None, ALU.mult)
                ins.then_inc(p_ready, 1)

            def take_probs(i, g):
                dve.wait_ge(turned, 6 * i + (3 * g + 2))
                await_count(dve, pv_done, 2 * i + g)
                nc.vector.tensor_copy(probsT[:, 1, :, :],
                                      sa[:, 0, :].rearrange("p (h q) -> p h q", h=GROUP)).then_inc(pt_dve, 1)

            def take_output(i, at):
                dve.wait_ge(pv_done, 2 * i + 2)
                nc.vector.tensor_copy(qT[:, :, at], pv[:, :].rearrange("p (c q) -> p c q", c=AC)).then_inc(o_taken, 1)

            def merge_a(i, window, mask_at, before, after):
                if before is not None:
                    take_output(i - 1, before)
                link(nc.vector.tensor_copy(vwin[:, :, 0, 0:HEAD], vtok[:, window, 0:HEAD]))
                nc.vector.tensor_copy(vwin[:, :, 1, HEAD:P], vtok[:, window, HEAD:P]).then_inc(v_staged, 1)
                softmax_tail(i, 0)
                take_probs(i, 0)
                softmax_head(i, 1, mask_at)
                softmax_tail(i, 1)
                if after is not None:
                    stage_q(after)
                take_probs(i, 1)

            def gate_up_a(i):
                dve.wait_ge(tile_done, 2 * i + (T_MA + 2))
                dve.wait_ge(drained[0], i + (T_MA // 2 + 1))
                at = i if isinstance(i, int) else bass.ds(i, 1)
                nc.vector.tensor_tensor(merged[:, at, :], sig, pm[:, 1, :], ALU.mult).then_inc(drained[1], 1)

            LINKS_A = 10
            dve.wait_ge(v_made, 2)
            stage_q(slice(0, P))
            conv_tiles(AC - 1)
            softmax_head(0, 0, 2 * P)
            conv_z(AC - 1)
            merge_a(0, slice(0, 3), 2 * P, None, slice(P, 2 * P))
            with chain.loop(1, NB - 1, LINKS_A) as i:
                softmax_head(i, 0, P)
                gate_up_a(i - 1)
                merge_a(i, bass.ds(i - 1, 3), P, bass.ds((i - 1) * P, P), bass.ds((i + 1) * P, P))
            softmax_head(NB - 1, 0, 0)
            gate_up_a(NB - 2)
            merge_a(NB - 1, slice(NB - 3, NB), 0, slice((NB - 2) * P, (NB - 1) * P), None)
            take_output(NB - 1, slice((NB - 1) * P, SEQ))
            gate_up_a(NB - 1)
            dve.wait_ge(o_taken, NB)

            def gated(i, q, t0, n0):
                p = q
                dve.wait_ge(sig_made, 2 * i + (n0 + q + 1))
                nc.vector.tensor_tensor(sig, pm[:, p, :], sig, ALU.mult).then_inc(drained[p], 1)
                dve.wait_ge(drained[p], i + ((t0 + q) // 2 + 1))
                at = bass.ds(2 * i + q, 1)
                nc.vector.tensor_tensor(sig, qT[:, at, :], sig, ALU.mult).then_inc(y_made, 1)
                dve.wait_ge(y_hi_made, 2 * i + (n0 + q + 1))
                nc.vector.tensor_tensor(y_lo[:, at, :], sig, y_hi[:, at, :].bitcast(F32),
                                        ALU.subtract).then_inc(y_ready, 1)
                dve.wait_ge(y_ready, 2 * i + (n0 + q + 1))

            with dve.Fori(0, AC // 2) as i:
                for q in range(2):
                    gated(i, q, T_ZB, AC)
            dve.wait_ge(mem_landed, 32)
            for b in range(2):
                link(nc.vector.tensor_tensor_reduce(out=area_a[:, MNH0 + b * D:MNH0 + (b + 1) * D],
                                                    in0=memx[:, b, :], in1=memx[:, b, :], scale=1.0, scalar=0.0,
                                                    op0=ALU.mult, op1=ALU.add, accum_out=st[:, 0, b:b + 1]))
            nc.vector.tensor_scalar(st[:, 1, 0:2], st[:, 0, 0:2], 1.0 / D, EPS, ALU.mult, ALU.add).then_inc(var_made, 1)
            dve.wait_ge(var_made, 5)
            dve.wait_ge(root_made, 5)
            inv_root(st[:, 1, 0:2], st[:, 2, 0:2], st[:, 9, 0:2], st[:, 10, 0:2])
            for b in range(2):
                ins = nc.vector.tensor_scalar(memx[:, b, :], memx[:, b, :], st[:, 9, b:b + 1], None, ALU.mult)
            ins.then_inc(memx_ready, 1)
            def take_mq(q):
                dve.wait_ge(tile_done, T_MQ + q + 1)
                nc.vector.tensor_copy(qT[:, q, :], pm[:, q % 2, :]).then_inc(drained[q % 2], 1)

            take_mq(0)
            take_mq(1)
            for n in range(4):
                dve.wait_ge(mem_turned, n + 1)
                bank = [sa[:, 0, :], sa[:, 1, :], sa[:, 2, :], pv[:, :]][n]
                for kk in range(2):
                    k, part = 2 * n + kk, bank[:, kk * MEM:(kk + 1) * MEM]
                    link(nc.vector.tensor_scalar(mn_hi[:, k, :], part, gmem[:, k:k + 1], None, ALU.mult))
                    ins = nc.vector.scalar_tensor_tensor(out=mn_lo[:, k, :], in0=part, scalar=gmem[:, k:k + 1],
                                                         in1=mn_hi[:, k, :].bitcast(F32), op0=ALU.mult,
                                                         op1=ALU.subtract)
                ins.then_inc(mn_made, 1)

            def memory_low(n):
                width = AW if n == T_MB + 1 - T_MEM else D
                dve.wait_ge(lo_made, T_MEM + n)
                dve.wait_ge(hi_made, T_MEM + n + 1)
                nc.vector.tensor_tensor(w_lo[:, n % 2, 0:width], raw[:, n % 2, 0:width],
                                        w_hi[:, n % 2, 0:width].bitcast(F32), ALU.subtract).then_inc(lo_made, 1)

            take_mq(2)
            memory_low(0)
            take_mq(3)
            for n in range(1, 2 * MHEADS + 1):
                memory_low(n)
            for p in range(2):
                dve.wait_ge(drained[p], T_MEM // 2)
            dve.wait_ge(tile_done, T_MB)

            def stage_mq(at):
                nc.vector.tensor_copy(mqz, qT[:, :, at]).then_inc(mq_staged, 1)

            def merge_in(i, t0, n0):
                dve.wait_ge(tile_done, 2 * i + (t0 + 2))
                dve.wait_ge(drained[0], i + (t0 // 2 + 1))
                nc.vector.tensor_tensor(sig, sig, pm[:, 1, :], ALU.mult).then_inc(drained[1], 1)
                dve.wait_ge(drained[1], i + (t0 // 2 + 1))
                at = i if isinstance(i, int) else bass.ds(i, 1)
                nc.vector.tensor_tensor(merged[:, at, :], merged[:, at, :], sig, ALU.add).then_inc(merged_done, 1)

            def merge_b(i, here, after):
                for b in range(2):
                    dve.wait_ge(mscored, 2 * i + (b + 1))
                    link(nc.vector.tensor_reduce(st[:, 0, 2 * b:2 * b + 2],
                                                 sa[:, b, :].rearrange("p (h m) -> p h m", h=2), AX.X, ALU.max))
                nc.vector.tensor_scalar(st[:, 3, 0:4], st[:, 0, 0:4], -float(P) ** -0.5, None,
                                        ALU.mult).then_inc(mnm_ready, 1)
                if after is not None:
                    stage_mq(after)
                dve.wait_ge(mexped, i + 1)
                link(nc.vector.reciprocal(st[:, 6, 0:4], st[:, 5, 0:4]))
                for h in range(MHEADS):
                    ins = nc.vector.tensor_scalar(mprobs[:, h, :], mprobs[:, h, :], st[:, 6, h:h + 1], None, ALU.mult)
                ins.then_inc(mp_ready, 1)
                dve.wait_ge(mturned, 2 * i + 2)
                dve.wait_ge(pv_done, i + 2 * NB)
                nc.vector.tensor_copy(mprobsT[:, 1, :, :],
                                      sa[:, 1, :].rearrange("p (h q) -> p h q", h=MHEADS)).then_inc(pt_dve, 1)
                merge_in(i, T_MB, 0)
                dve.wait_ge(pv_done, i + (2 * NB + 1))
                nc.vector.tensor_copy(qT[:, :, here], pv[:, :].rearrange("p (h q) -> p h q", h=MHEADS)).then_inc(o_taken, 1)

            LINKS_B = 3
            stage_mq(slice(0, P))
            memory_low(2 * MHEADS + 1)
            with chain.loop(0, NB - 1, LINKS_B) as i:
                merge_b(i, bass.ds(i * P, P), bass.ds((i + 1) * P, P))
            merge_b(NB - 1, slice((NB - 1) * P, SEQ), None)
            dve.wait_ge(o_taken, 2 * NB)
            dve.wait_ge(merged_done, KC)

            with dve.Fori(0, AC // 2) as i:
                for q in range(2):
                    gated(i, q, T_ZM, 2 * AC)
            with dve.Fori(0, KC - 1) as i:
                merge_in(i, T_MM, KC)

            def wout_low(half):
                for k in range(KC):
                    n = half * KC + k
                    dve.wait_ge(wo_hi_made, n + 1)
                    nc.vector.tensor_tensor(wo_lo[:, n * HALF:(n + 1) * HALF], wout_raw[:, n * HALF:(n + 1) * HALF],
                                            wo_hi[:, n * HALF:(n + 1) * HALF].bitcast(F32),
                                            ALU.subtract).then_inc(wo_lo_made, 1)

            def merged_low(p, at, b1):
                dve.wait_ge(mb_hi_made, b1)
                nc.vector.tensor_tensor(mb_lo[:, p * D:(p + 1) * D].rearrange("p (k q) -> p k q", k=KC), at,
                                        mb_hi[:, p * D:(p + 1) * D].bitcast(F32).rearrange("p (k q) -> p k q", k=KC),
                                        ALU.subtract).then_inc(mb_lo_made, 1)

            wout_low(0)
            dve.wait_ge(drained[0], T_OUT // 2)
            for half in range(2):
                cols = slice(half * HALF, (half + 1) * HALF)
                if half == 0:
                    dve.wait_ge(up_half_done, 3 * KC)
                    link(nc.vector.tensor_tensor(sig[:, cols], sig[:, cols], pm[:, 1, cols], ALU.mult))
                else:
                    dve.wait_ge(tile_done, T_OUT)
                    nc.vector.tensor_tensor(sig[:, cols], sig[:, cols], pm[:, 1, cols], ALU.mult).then_inc(drained[1], 1)
                    dve.wait_ge(drained[1], T_OUT // 2)
                nc.vector.tensor_tensor(merged[:, KC - 1, cols], merged[:, KC - 1, cols], sig[:, cols],
                                        ALU.add).then_inc(merged_done, 1)
                if half == 0:
                    merged_low(0, merged[:, :, 0:P], 1)
            wout_low(1)
            merged_low(1, merged[:, :, P:2 * P], 2)

            dve.wait_ge(gpost_landed, 16)

            def out_block(i, p, more):
                dve.wait_ge(sq_made, 2 * i + (p + 1))
                var, root, r, t = (st[:, n, p:p + 1] for n in (7, 8, 9, 10))
                nc.vector.tensor_scalar(var, st[:, 6, p:p + 1], 1.0 / D, EPS, ALU.mult, ALU.add).then_inc(out_var, 1)
                dve.wait_ge(out_var, 2 * i + (p + 1))
                if more:
                    merged_low(p, merged[:, :, bass.ds((2 * i + (p + 2)) * P, P)], 2 * i + (p + 3))
                dve.wait_ge(out_root, 2 * i + (p + 1))
                inv_root(var, root, r, t)
                nc.vector.scalar_tensor_tensor(out=tout[:, p, :], in0=pm[:, p, :], scalar=r, in1=gpostb,
                                               op0=ALU.mult, op1=ALU.mult).then_inc(drained[p], 1)
                dve.wait_ge(drained[p], i + (T_OUT // 2 + 1))
                dve.wait_ge(xres_landed[p], 16 * i + 16)
                nc.vector.tensor_tensor(tout[:, p, :], tout[:, p, :], raw[:, p, :], ALU.add).then_inc(out_ready, 1)

            with chain.loop(0, NB // 2 - 1, 10) as i:
                for p in range(2):
                    out_block(i, p, True)
            for p in range(2):
                out_block(NB // 2 - 1, p, False)


def _units(np_, w, order):
    rows = w.shape[0]
    u = w.reshape(rows // P, P, w.shape[1] // P, P)[:, :, order, :]
    return np_.ascontiguousarray(u.transpose(2, 1, 0, 3)).reshape(len(order), P, rows)


def _tables():
    half = ROT // 2
    inv = np.power(np.float64(ROPE_THETA), -np.arange(half) * (2.0 / ROT)).astype(np.float32)
    ang = (np.arange(SEQ, dtype=np.float32)[None, :] * inv[:, None]).astype(np.float64)
    cos, sin = np.ones((P, SEQ), np.float32), np.zeros((P, SEQ), np.float32)
    for row in (0, HEAD):
        cos[row:row + half] = cos[row + half:row + ROT] = np.cos(ang)
        sin[row:row + half], sin[row + half:row + ROT] = -np.sin(ang), np.sin(ang)
    q, k = np.arange(P)[:, None], np.arange(P)[None, :]
    none = np.full((P, P), -1e30, np.float32)
    left = np.where(k >= q, 0, none).astype(np.float32)
    right = np.where(k <= q, 0, none).astype(np.float32)
    strip = np.concatenate([none, left, np.zeros((P, P), np.float32), right, none], axis=1)
    return cos, sin, strip, np.eye(P, dtype=np.float32)


def kernel(x, mem, g_pre, w_in, w_conv, attn_sink, g_mem, w_mem_kv, w_up_a, w_up_b, w_up_m, w_out, g_post):
    import concourse.bacc as bacc
    from concourse.bass_utils import run_bass_kernel_spmd as run

    w_in = np.asarray(w_in)[0]
    pair = np.concatenate([np.r_[c * HEAD:(c + 1) * HEAD, (c + GROUP) * HEAD:(c + GROUP + 1) * HEAD]
                           for c in range(AC)])
    start = np.cumsum([0, AW, AW, AW, AW, AW, P, P, AW, AW, AW])
    a_b, a_c, a_x, a_z, b_q, b_k, b_v, b_z, m_q, m_z, gates = start
    cols = [np.arange(b_k, b_k + P), np.arange(b_v, b_v + P), b_q + pair]
    for c in range(AC):
        cols += [np.arange(s + c * P, s + (c + 1) * P) for s in (a_c, a_x, a_b, a_z)]
    cols += [np.arange(gates, gates + D), b_z + pair, np.arange(m_q, m_q + AW),
             np.arange(gates + D, gates + 2 * D), np.arange(m_z, m_z + AW),
             np.arange(gates + 2 * D, gates + 3 * D)]
    w8 = _units(np, w_in[:, np.concatenate(cols)], np.arange(w_in.shape[1] // P))
    wup = np.concatenate([_units(np, w, np.arange(KC)) for w in
                          (np.asarray(w_up_a)[0], np.asarray(w_up_b)[0][pair], np.asarray(w_up_m)[0])])
    w_kv = np.asarray(w_mem_kv)[0]
    wmem = np.concatenate([_units(np, w_kv, np.arange(MHEADS)),
                           w_kv[:, AW:].reshape(MHEADS, 2, P, AW).transpose(0, 2, 1, 3).reshape(MHEADS, P, D)])
    wout = np.ascontiguousarray(np.asarray(w_out)[0].reshape(KC, P, 2, HALF).transpose(2, 1, 0, 3)
                                ).reshape(2, P, KC * HALF)
    cos, sin, strip, eye = _tables()

    def columns(g):
        return np.ascontiguousarray(np.asarray(g)[0].reshape(-1, P).T)

    arrays = {
        "x": np.asarray(x)[0], "mem": np.asarray(mem)[0], "w8": w8, "wup": wup, "wmem": wmem, "wout": wout,
        "g_pre": columns(g_pre), "g_mem": columns(g_mem),
        "g_post": np.ascontiguousarray(np.broadcast_to(np.asarray(g_post)[0], (P, D))),
        "w_conv": np.ascontiguousarray(np.asarray(w_conv)[0].reshape(3, AC, P).transpose(2, 0, 1)),
        "sink": np.ascontiguousarray(np.broadcast_to(np.asarray(attn_sink)[0], (P, HEADS))),
        "cos": cos, "sin": sin, "mask": strip, "ident": eye,
    }
    nc = bacc.Bacc("TRN2", target_bir_lowering=False, num_devices=1)
    ins = [nc.dram_tensor(f"in_{n}", a.shape, F32, kind="ExternalInput").ap() for n, a in arrays.items()]
    out = nc.dram_tensor("out_0", (SEQ, D), F32, kind="ExternalOutput").ap()
    hybrid_layer(nc, *ins, out)
    r = run(nc, [{f"in_{n}": np.ascontiguousarray(a) for n, a in arrays.items()}], core_ids=[0])
    return r.results[0]["out_0"].reshape(1, SEQ, D)
```

```python
from contextlib import ExitStack, contextmanager

import numpy as np

import concourse.bass as bass
from concourse import mybir

P = 128
D = 1024
SEQ = 1024
KC = D // P
NB = SEQ // P
HALF = 512
AW = D // 2
AC = AW // P
HEAD = 64
GROUP = 4
HEADS = 8
MEM = 256
MHEADS = 4
WIN = 3 * P
EPS = 1e-6
ROPE_THETA = 500000.0
ROT = HEAD // 4
BANKS = (2, 0, 1)

F32 = mybir.dt.float32
F32R = mybir.dt.float32r
ALU = mybir.AluOpType
ACT = mybir.ActivationFunctionType
AX = mybir.AxisListType

T_QKV = 0
T_CONV = T_QKV + 2 + AC
T_MA = T_CONV + 4 * AC
T_ZB = T_MA + 2 * KC
T_MQ = T_ZB + AC
T_MEM = T_MQ + AC
T_MB = T_MEM + 2 * MHEADS
T_ZM = T_MB + 2 * KC
T_MM = T_ZM + AC
T_OUT = T_MM + 2 * KC

Q0, K0, V0, QZ0, P0, PT0, VW0 = 0, 4096, 5120, 6144, 7168, 8704, 10240
SIG0, KWL0, VWL0, AREA_A = 11008, 12032, 12416, 13184
MK0, MV0, MX0, MNH0, MNL0 = 4096, 5120, 6144, 8192, 10240
MKL0, MPT0, MP0, MQH0, MQL0 = 6144, 7168, 8192, 9216, 9728
GP0, TO0 = 8192, 9216
QRAW0, SWAP0, COS0, SIN0, ROT0, VT0 = 0, 1024, 2048, 3072, 4096, 5120
CU0, TA0, CS0 = 2048, 4096, 5120
QL0, KWH0 = 6144, 7168


def await_count(eng, sem, count):
    if not (isinstance(count, int) and count == 0):
        eng.wait_ge(sem, count)


class Chain:

    def __init__(self, eng, sem):
        self.eng, self.sem, self.base, self.inside, self.turn = eng, sem, 0, 0, None

    def link(self, ins):
        self.inside += 1
        ins.then_inc(self.sem, 1)
        at = self.base + self.inside
        if self.turn is not None:
            i, first, per = self.turn
            at = (i - first) * per + at if first else i * per + at
        self.eng.wait_ge(self.sem, at)

    @contextmanager
    def loop(self, first, end, per):
        self.base, self.inside = self.base + self.inside, 0
        with self.eng.Fori(first, end) as i:
            self.turn = (i, first, per)
            yield i
        assert self.inside == per, (self.inside, per)
        self.base, self.inside, self.turn = self.base + per * (end - first), 0, None


def hybrid_layer(nc, x, mem, w8, wup, wmem, wout, g_pre, g_mem, g_post, w_conv, sink,
                 cos, sin, mask, ident_in, out):
    ctx = ExitStack()
    with ctx:
        def sb(name, shape, dt=F32):
            return ctx.enter_context(nc.sbuf_tensor(name, shape, dt))

        def psum(name, shape):
            return ctx.enter_context(nc.psum_tensor(name, shape, F32))

        def sem(name):
            return ctx.enter_context(nc.semaphore(name))

        h_hi = sb("h_hi", [P, KC, SEQ], F32R)
        h_lo = sb("h_lo", [P, KC, SEQ], F32R)
        y_hi = sb("y_hi", [P, AC, SEQ], F32R)
        y_lo = sb("y_lo", [P, AC, SEQ], F32R)

        def two_names(name, shape):
            with nc.sbuf_tensor(name, shape, F32) as as_f32:
                pass
            return as_f32, sb(name + "_r", shape, F32R)

        area_m, area_mr = two_names("area_m", [P, KC * SEQ])
        area_a, area_r = two_names("area_a", [P, AREA_A])
        units, units_r = two_names("units", [P, 3, 2, D])
        raw, w_hi, w_lo = units[:, 0, :, :], units_r[:, 1, :, :], units_r[:, 2, :, :]
        maskb = sb("maskb", [P, 5 * P])
        ident = sb("ident", [P, P])
        gpre = sb("gpre", [P, KC])
        gmem = sb("gmem", [P, KC])
        wconv = sb("wconv", [P, 3, AC])
        sinkb = sb("sinkb", [P, HEADS])
        st = sb("st", [P, 12, 8])

        merged = area_m[:, :].rearrange("p (k s) -> p k s", k=KC)
        qT = area_a[:, Q0:K0].rearrange("p (c s) -> p c s", c=AC)
        kT = area_a[:, K0:K0 + SEQ]
        vtok = area_a[:, V0:V0 + SEQ].rearrange("p (b d) -> p b d", b=NB)
        q_stack = area_r[:, QZ0:QZ0 + 2 * GROUP * P].rearrange("p (g h q) -> p g h q", g=2, h=GROUP)
        q_stack_f32 = q_stack.bitcast(F32)
        q_low = area_m[:, QL0:QL0 + GROUP * P].rearrange("p (h q) -> p h q", h=GROUP)
        k_hi = area_mr[:, KWH0:KWH0 + 2 * WIN].rearrange("p (g k) -> p g k", g=2)
        k_lo = area_r[:, KWL0:KWL0 + WIN]
        probs = area_a[:, P0:P0 + GROUP * WIN].rearrange("p (h k) -> p h k", h=GROUP)
        probsT_hi = area_r[:, PT0:PT0 + 3 * GROUP * P].rearrange("p (j n) -> p j n", j=3)
        probsT_lo = units_r[:, :, 1, AW:D]
        vwin_hi = area_r[:, VW0:VW0 + 3 * 2 * P].rearrange("p (j g d) -> p j g d", j=3, g=2)
        vwin_lo = area_r[:, VWL0:VWL0 + 3 * 2 * P].rearrange("p (j g d) -> p j g d", j=3, g=2)
        sig = area_a[:, SIG0:SIG0 + SEQ]
        conv_c = area_m[:, CS0:CS0 + SEQ]
        conv_cu = area_m[:, CU0:CU0 + SEQ + 2]
        conv_t = area_m[:, TA0:TA0 + SEQ]
        q_raw = area_m[:, QRAW0:QRAW0 + SEQ]
        q_swap = area_m[:, SWAP0:SWAP0 + SEQ]
        cosb = area_m[:, COS0:COS0 + SEQ]
        sinb = area_m[:, SIN0:SIN0 + SEQ]
        rot_t = area_m[:, ROT0:ROT0 + SEQ]
        vT = area_m[:, VT0:VT0 + SEQ]
        mk_hi = area_r[:, MK0:MK0 + MHEADS * MEM].rearrange("p (h m) -> p h m", h=MHEADS)
        mk_lo = area_r[:, MKL0:MKL0 + MHEADS * MEM].rearrange("p (h m) -> p h m", h=MHEADS)
        mv = area_a[:, MV0:MV0 + 2 * AW].rearrange("p (b d) -> p b d", b=2)
        memx = area_a[:, MX0:MX0 + 2 * D].rearrange("p (b d) -> p b d", b=2)
        mn_hi = area_r[:, MNH0:MNH0 + KC * MEM].rearrange("p (k m) -> p k m", k=KC)
        mn_lo = area_r[:, MNL0:MNL0 + KC * MEM].rearrange("p (k m) -> p k m", k=KC)
        mprobs = area_a[:, MP0:MP0 + MHEADS * MEM].rearrange("p (h m) -> p h m", h=MHEADS)
        mprobsT = area_a[:, MPT0:MPT0 + 2 * MHEADS * P].rearrange("p (b h q) -> p b h q", b=2, h=MHEADS)
        mq_hi = area_r[:, MQH0:MQH0 + MHEADS * P].rearrange("p (h q) -> p h q", h=MHEADS)
        mq_lo = area_r[:, MQL0:MQL0 + MHEADS * P].rearrange("p (h q) -> p h q", h=MHEADS)
        wout_raw = area_a[:, 0:KC * D]
        gpostb = area_a[:, GP0:GP0 + D]
        squares = area_a[:, 0:2 * D].rearrange("p (b d) -> p b d", b=2)
        tout = area_a[:, TO0:TO0 + 2 * D].rearrange("p (b d) -> p b d", b=2)
        wo_hi = h_hi[:, :, :].rearrange("p k s -> p (k s)")
        wo_lo = h_lo[:, :, :].rearrange("p k s -> p (k s)")
        mb_hi = w_hi.rearrange("p b d -> p (b d)")
        mb_lo = w_lo.rearrange("p b d -> p (b d)")

        pm = psum("pm", [P, 2, SEQ])
        sa = psum("sa", [P, 3, HALF])
        pv = psum("pv", [P, HALF])

        x_landed = [sem(f"x_landed{b}") for b in range(NB)]
        ident_landed = sem("ident_landed")
        small_landed = sem("small_landed")
        st_cleared = sem("st_cleared")
        rope_landed = sem("rope_landed")
        mem_landed = sem("mem_landed")
        gpost_landed = sem("gpost_landed")
        wout_landed = [sem(f"wout_landed{n}") for n in range(2)]
        raw_landed = [sem(f"raw_landed{p}") for p in range(2)]
        xres_landed = [sem(f"xres_landed{p}") for p in range(2)]
        stored = [sem(f"stored{p}") for p in range(2)]
        ssq_act = sem("ssq_act")
        var_made, root_made, xs_made = sem("var_made"), sem("root_made"), sem("xs_made")
        x_turned, h_hi_made, h_made = sem("x_turned"), sem("h_hi_made"), sem("h_made")
        hi_made, lo_made = sem("hi_made"), sem("lo_made")
        tile_done = sem("tile_done")
        up_half_done = sem("up_half_done")
        drained = [sem(f"drained{p}") for p in range(2)]
        swapped, roped = sem("swapped"), sem("roped")
        v_turned, v_made = sem("v_turned"), sem("v_made")
        sig_made, y_made, y_hi_made, y_ready = sem("sig_made"), sem("y_made"), sem("y_hi_made"), sem("y_ready")
        qk_moved = sem("qk_moved")
        qk_staged, v_staged = sem("qk_staged"), sem("v_staged")
        scored, masked, nm_ready, exped = sem("scored"), sem("masked"), sem("nm_ready"), sem("exped")
        p_ready, turned, pt_hi_made, pt_lo_made = sem("p_ready"), sem("turned"), sem("pt_hi_made"), sem("pt_lo_made")
        pv_done, o_taken = sem("pv_done"), sem("o_taken")
        memx_ready, mem_turned, mn_made = sem("memx_ready"), sem("mem_turned"), sem("mn_made")
        mq_staged, mscored, mnm_ready, mexped = sem("mq_staged"), sem("mscored"), sem("mnm_ready"), sem("mexped")
        mk_hi_made = sem("mk_hi_made")
        mp_ready, mturned, merged_done = sem("mp_ready"), sem("mturned"), sem("merged_done")
        wo_hi_made, wo_lo_made = sem("wo_hi_made"), sem("wo_lo_made")
        mb_hi_made, mb_lo_made = sem("mb_hi_made"), sem("mb_lo_made")
        out_half_done = sem("out_half_done")
        sq_made, out_var, out_root, out_ready = sem("sq_made"), sem("out_var"), sem("out_root"), sem("out_ready")
        act_chain, dve_chain = sem("act_chain"), sem("dve_chain")

        block = ctx.enter_context(nc.Block())

        @block.sync
        def _(sp):
            for b in range(NB):
                sp.dma_start(area_m[:, b * D:(b + 1) * D], x[b * P:(b + 1) * P, :]).then_inc(x_landed[b], 16)
                if b == 3:
                    sp.dma_start(ident[:, :], ident_in).then_inc(ident_landed, 16)
                    sp.dma_start(gpre[:, :], g_pre).then_inc(ident_landed, 16)
                    sp.dma_start(raw[:, 0, :], w8[0]).then_inc(raw_landed[0], 16)
            sp.dma_start(raw[:, 1, :], w8[1]).then_inc(raw_landed[1], 16)
            for dst, src in ((gmem[:, :], g_mem), (wconv[:, :, :], w_conv), (sinkb[:, :], sink), (maskb[:, :], mask)):
                sp.dma_start(dst, src).then_inc(small_landed, 16)
            sp.wait_ge(x_turned, 8)
            sp.dma_start(cosb, cos).then_inc(rope_landed, 16)
            sp.dma_start(sinb, sin).then_inc(rope_landed, 16)

            with sp.Fori(1, T_MA // 2) as i:
                for p in range(2):
                    sp.wait_ge(lo_made, 2 * i + (p - 1))
                    sp.dma_start(raw[:, p, :], w8[2 * i + p]).then_inc(raw_landed[p], 16)

            def merge_loads(sp, i, t0, w8_0, up0):
                sp.wait_ge(lo_made, 2 * i + (t0 - 1))
                sp.dma_start(raw[:, 0, :], w8[i + w8_0]).then_inc(raw_landed[0], 16)
                sp.wait_ge(lo_made, 2 * i + t0)
                sp.dma_start(raw[:, 1, 0:AW], wup[i + up0]).then_inc(raw_landed[1], 16)

            def move_qk(i):
                sp.wait_ge(qk_staged, i + 1)
                for g in range(2):
                    own, other = slice(g * HEAD, (g + 1) * HEAD), slice((1 - g) * HEAD, (2 - g) * HEAD)
                    sp.dma_start(q_stack_f32[other, g, :, :], q_low[own, :, :]).then_inc(qk_moved, 16)
                    sp.dma_start(k_hi[other, g, :].bitcast(F32), k_hi[own, g, :].bitcast(F32)).then_inc(qk_moved, 16)

            move_qk(0)
            for i in range(2):
                merge_loads(sp, i, T_MA, T_MA, 0)
            with sp.Fori(2, KC) as i:
                move_qk(i - 1)
                merge_loads(sp, i, T_MA, T_MA, 0)
            move_qk(NB - 1)
            n8 = T_MA + KC
            sp.wait_ge(lo_made, T_ZB - 1)
            sp.dma_start(raw[:, 0, :], w8[n8]).then_inc(raw_landed[0], 16)
            sp.wait_ge(lo_made, T_ZB)
            sp.wait_ge(pv_done, 2 * NB)
            sp.dma_start(raw[:, 1, :], w8[n8 + 1]).then_inc(raw_landed[1], 16)
            with sp.Fori(1, AC) as i:
                for p in range(2):
                    sp.wait_ge(lo_made, 2 * i + (T_ZB + p - 1))
                    sp.dma_start(raw[:, p, :], w8[2 * i + (n8 + p)]).then_inc(raw_landed[p], 16)
            n8 += 2 * AC
            sp.wait_ge(pv_done, 2 * NB)
            for b in range(2):
                sp.dma_start(memx[:, b, :], mem[b * P:(b + 1) * P, :]).then_inc(mem_landed, 16)
            with sp.Fori(0, MHEADS) as i:
                for p in range(2):
                    sp.wait_ge(lo_made, 2 * i + (T_MEM + p - 1))
                    sp.dma_start(raw[:, p, :], wmem[2 * i + p]).then_inc(raw_landed[p], 16)
            with sp.Fori(0, KC) as i:
                merge_loads(sp, i, T_MB, n8, KC)
            n8 += KC
            with sp.Fori(0, AC // 2) as i:
                for p in range(2):
                    sp.wait_ge(lo_made, 2 * i + (T_ZM + p - 1))
                    sp.dma_start(raw[:, p, :], w8[2 * i + (n8 + p)]).then_inc(raw_landed[p], 16)
            n8 += AC
            with sp.Fori(0, KC) as i:
                merge_loads(sp, i, T_MM, n8, 2 * KC)
            sp.wait_ge(y_ready, 3 * AC)
            for n in range(2):
                sp.dma_start(wout_raw[:, n * KC * HALF:(n + 1) * KC * HALF], wout[n]).then_inc(wout_landed[n], 16)
            sp.dma_start(gpostb, g_post).then_inc(gpost_landed, 16)
            sp.wait_ge(lo_made, T_OUT)
            for p in range(2):
                sp.dma_start(raw[:, p, :], x[p * P:(p + 1) * P, :]).then_inc(xres_landed[p], 16)
            with sp.Fori(0, NB // 2 - 1) as i:
                for p in range(2):
                    sp.wait_ge(out_ready, 2 * i + (p + 1))
                    sp.dma_start(out[bass.ds((2 * i + p) * P, P), :], tout[:, p, :]).then_inc(stored[p], 16)
                    sp.dma_start(raw[:, p, :], x[bass.ds((2 * i + (p + 2)) * P, P), :]).then_inc(xres_landed[p], 16)
            sp.wait_ge(out_ready, NB - 1)
            sp.dma_start(out[SEQ - 2 * P:SEQ - P, :], tout[:, 0, :]).then_inc(stored[0], 16)
            for half in range(2):
                sp.wait_ge(out_ready, NB + half)
                cols = slice(half * HALF, (half + 1) * HALF)
                sp.dma_start(out[SEQ - P:SEQ, cols], tout[:, 1, cols]).then_inc(stored[1], 16)
            sp.wait_ge(stored[0], 16 * (NB // 2))
            sp.wait_ge(stored[1], 16 * (NB // 2 + 1))

        @block.gpsimd
        def _(pool):
            def low_part(p, nth, width=D):
                pool.wait_ge(hi_made, nth)
                nc.gpsimd.tensor_tensor(w_lo[:, p, 0:width], raw[:, p, 0:width], w_hi[:, p, 0:width].bitcast(F32),
                                        ALU.subtract).then_inc(lo_made, 1)

            low_part(0, 1)
            pool.wait_ge(x_turned, 8)
            nc.gpsimd.memset(q_swap, 0.0).then_inc(rope_landed, 16)
            low_part(1, 2)
            for t0, end, width in ((2, T_MA, D), (T_MA, T_ZB, AW), (T_ZB, T_MEM, D),
                                   (T_MB + 2, T_ZM, AW), (T_ZM, T_MM, D), (T_MM, T_OUT, AW)):
                if t0 == T_MB + 2:
                    pool.wait_ge(lo_made, t0)
                with pool.Fori(t0 // 2, end // 2) as i:
                    low_part(0, 2 * i + 1)
                    low_part(1, 2 * i + 2, width)

        @block.tensor
        def _(pe):
            def product(t_half, p, chunks, src_hi, src_lo, nth, first=0, last=None, ready=None):
                last = 2 * chunks if last is None else last
                if first == 0:
                    await_count(pe, drained[p], t_half)
                for step in range(first, last):
                    half, k = divmod(step, chunks)
                    if ready is not None:
                        ready(step)
                    if step == 0:
                        pe.wait_ge(hi_made, nth)
                        pe.wait_ge(lo_made, nth)
                    cols = slice(half * HALF, (half + 1) * HALF)
                    hi, lo = w_hi[:, p, k * P:(k + 1) * P], w_lo[:, p, k * P:(k + 1) * P]
                    pe.matmul(pm[:, p, cols], hi, src_hi[:, k, cols], start=(k == 0), stop=False)
                    pe.matmul(pm[:, p, cols], hi, src_lo[:, k, cols], start=False, stop=False)
                    mm = pe.matmul(pm[:, p, cols], lo, src_hi[:, k, cols], start=False, stop=(k == chunks - 1))
                    if step == 2 * chunks - 1:
                        mm.then_inc(tile_done, 1)
                    elif k == chunks - 1 and chunks == AC:
                        mm.then_inc(up_half_done, 1)

            def from_h(i, t0, q=0, first=0, last=None, ready=None):
                product((t0 + q) // 2 + i, q % 2, KC, h_hi, h_lo, 2 * i + (t0 + q + 1),
                        first, last, ready)

            def from_y(i, t0, first=0, last=None):
                product(t0 // 2 + i, 1, AC, y_hi, y_lo, 2 * i + (t0 + 2), first, last)

            spare = [sa[:, 0, :], sa[:, 1, :], sa[:, 2, :], pv[:, :]]

            def turn_x(n, pairs=(0, 1)):
                half, k = divmod(n, KC)
                if n >= 4 and pairs[0] == 0:
                    pe.wait_ge(h_made, n - 3)
                for b in [2 * pair + b for pair in pairs for b in range(2)]:
                    src = area_m[:, (4 * half + b) * D + k * P:(4 * half + b) * D + (k + 1) * P]
                    mm = pe.transpose(spare[n % 4][:, b * P:(b + 1) * P], src, ident[:, :])
                if pairs[-1] == 1:
                    mm.then_inc(x_turned, 1)

            def turn_then_wait(step):
                if step == 0:
                    for pair in range(2):
                        pe.wait_ge(xs_made, pair + 1)
                        for n in range(4):
                            turn_x(n, (pair,))
                elif step + 3 < 2 * KC:
                    if step + 3 == KC:
                        pe.wait_ge(xs_made, 4)
                    turn_x(step + 3)
                pe.wait_ge(h_made, step + 1)

            pe.wait_ge(ident_landed, 32)
            for q in range(2 + AC):
                p = q % 2
                from_h(0, T_QKV, q, ready=turn_then_wait if q == 0 else None)
                if q == 2:
                    pe.wait_ge(drained[1], 1)
                    for n in range(2):
                        for b in range(4):
                            mm = pe.transpose(sa[:, n, b * P:(b + 1) * P],
                                              vT[:, (4 * n + b) * P:(4 * n + b + 1) * P], ident[:, :])
                        mm.then_inc(v_turned, 1)

            def conv_tile(j, q, first=0, last=None):
                product(2 * j + (T_CONV + q) // 2, q % 2, KC, h_hi, h_lo, 4 * j + (T_CONV + q + 1), first, last)

            with pe.Fori(0, AC - 1) as j:
                for q in range(4):
                    conv_tile(j, q)

            def scores(i, g):
                if g == 0:
                    pe.wait_ge(qk_moved, 64 * i + 64)
                own = slice(g * HEAD, (g + 1) * HEAD)
                for h in range(GROUP):
                    b = BANKS[h % 3]
                    if h < 3:
                        if isinstance(i, int) and i == g == 0:
                            pe.wait_ge(v_made, 2)
                        else:
                            pe.wait_ge(pt_lo_made, 6 * i + (3 * g + h - 2))
                    else:
                        pe.wait_ge(masked, 8 * i + (4 * g + 1))
                    pe.matmul(sa[:, b, 0:WIN], q_stack[:, g, h, :], k_hi[:, g, :], start=True, stop=False)
                    pe.matmul(sa[:, b, 0:WIN], q_stack[own, g, h, :], k_lo[own, :],
                              start=False, stop=True).then_inc(scored, 1)

            def turn_probs(i, g):
                pe.wait_ge(p_ready, 2 * i + (g + 1))
                for j, bank in enumerate(BANKS):
                    for h in range(GROUP):
                        mm = pe.transpose(sa[:, bank, h * P:(h + 1) * P], probs[:, h, j * P:(j + 1) * P], ident[:, :])
                    mm.then_inc(turned, 1)

            def values(i, g):
                if g == 0:
                    pe.wait_ge(v_staged, i + 1)
                    await_count(pe, o_taken, i)
                blocks = {0: (0, 1), NB - 1: (1, 2)}.get(i, (0, 1, 2)) if isinstance(i, int) else (0, 1, 2)
                for j in blocks:
                    pe.wait_ge(pt_hi_made, 6 * i + (3 * g + j + 1))
                    pe.wait_ge(pt_lo_made, 6 * i + (3 * g + j + 1))
                    for n, (v, pr) in enumerate(((vwin_hi, probsT_hi), (vwin_hi, probsT_lo), (vwin_lo, probsT_hi))):
                        mm = pe.matmul(pv[:, :], v[:, j, g, :], pr[:, j, :], start=(g == 0 and j == blocks[0] and n == 0),
                                       stop=(g == 1 and j == blocks[-1] and n == 2))
                mm.then_inc(pv_done, 1)

            def merge_a(i, first=False):
                if not first:
                    scores(i, 0)
                    values(i - 1, 1)
                n = 13 if first else 10
                from_h(i, T_MA, 0, 0, n)
                turn_probs(i, 0)
                from_h(i, T_MA, 0, n, n + 2)
                scores(i, 1)
                values(i, 0)
                from_h(i, T_MA, 0, n + 2)
                if first:
                    pe.wait_ge(y_ready, AC)
                from_y(i, T_MA, 0, 6)
                turn_probs(i, 1)
                from_y(i, T_MA, 6)

            for q in range(3):
                conv_tile(AC - 1, q)
            conv_tile(AC - 1, 3, 0, 3)
            scores(0, 0)
            conv_tile(AC - 1, 3, 3)
            merge_a(0, first=True)
            merge_a(1)
            with pe.Fori(2, NB - 1) as i:
                merge_a(i)
            merge_a(NB - 1)
            values(NB - 1, 1)

            with pe.Fori(0, AC // 2) as i:
                for q in range(2):
                    from_h(i, T_ZB, q)
            for q in range(AC):
                from_h(0, T_MQ, q)
                if q == 1:
                    pe.wait_ge(memx_ready, 1)
                    for n in range(4):
                        for kk in range(2):
                            for b in range(2):
                                k = 2 * n + kk
                                mm = pe.transpose(spare[n][:, kk * MEM + b * P:kk * MEM + (b + 1) * P],
                                                  memx[:, b, k * P:(k + 1) * P], ident[:, :])
                        mm.then_inc(mem_turned, 1)

            pe.wait_ge(mn_made, 4)
            parts = ((w_hi, mn_hi), (w_hi, mn_lo), (w_lo, mn_hi))
            for n in range(MHEADS):
                p, t = n % 2, T_MEM + n
                pe.wait_ge(drained[p], t // 2)
                pe.wait_ge(hi_made, t + 1)
                for which, (w, m) in enumerate(parts):
                    if which == 2:
                        pe.wait_ge(lo_made, t + 1)
                    for k in range(KC):
                        mm = pe.matmul(pm[:, p, 0:MEM], w[:, p, k * P:(k + 1) * P], m[:, k, :],
                                       start=(which == 0 and k == 0), stop=(which == 2 and k == KC - 1))
                mm.then_inc(tile_done, 1)
            pe.wait_ge(drained[1], (T_MEM + MHEADS) // 2)
            for n in range(MHEADS):
                p, t = n % 2, T_MEM + MHEADS + n
                pe.wait_ge(hi_made, t + 1)
                for which, (w, m) in enumerate(parts):
                    if which == 2:
                        pe.wait_ge(lo_made, t + 1)
                    for kk in range(2):
                        for b in range(2):
                            mm = pe.matmul(pm[:, 1, b * HALF:(b + 1) * HALF], m[:, 2 * n + kk, b * P:(b + 1) * P],
                                           w[:, p, kk * AW:(kk + 1) * AW],
                                           start=(n == 0 and which == 0 and kk == 0),
                                           stop=(n == MHEADS - 1 and which == 2 and kk == 1))
                            if n < MHEADS - 1 and which == 0 and kk == 0 and b == 0:
                                mm.then_inc(drained[p], 1)
                mm.then_inc(tile_done, 1)

            with pe.Fori(0, KC) as i:
                from_h(i, T_MB, 0, 0, 3)
                pe.wait_ge(mq_staged, i + 1)
                pe.wait_ge(drained[1], (T_MEM + 8) // 2)
                for b in range(2):
                    pe.wait_ge((pt_hi_made, pt_lo_made)[b], i + 6 * NB)
                    for h in range(2 * b, 2 * b + 2):
                        for n, (q, k) in enumerate(((mq_hi, mk_hi), (mq_hi, mk_lo), (mq_lo, mk_hi))):
                            mm = pe.matmul(sa[:, b, (h % 2) * MEM:(h % 2 + 1) * MEM], q[:, h, :], k[:, h, :],
                                           start=(n == 0), stop=(n == 2))
                    mm.then_inc(mscored, 1)
                from_h(i, T_MB, 0, 3)
                pe.wait_ge(mp_ready, i + 1)
                for b in range(2):
                    for h in range(MHEADS):
                        mm = pe.transpose(sa[:, b, h * P:(h + 1) * P], mprobs[:, h, b * P:(b + 1) * P], ident[:, :])
                    mm.then_inc(mturned, 1)
                pe.wait_ge(y_ready, 2 * AC)
                from_y(i, T_MB, 0, 6)
                pe.wait_ge(pt_hi_made, i + (6 * NB + 1))
                pe.wait_ge(pt_lo_made, i + (6 * NB + 1))
                pe.wait_ge(o_taken, i + NB)
                for h in range(MHEADS):
                    for b in range(2):
                        mm = pe.matmul(pv[:, h * P:(h + 1) * P], mv[:, b, h * P:(h + 1) * P], mprobsT[:, b, h, :],
                                       start=(b == 0), stop=(b == 1))
                mm.then_inc(pv_done, 1)
                from_y(i, T_MB, 6)

            with pe.Fori(0, AC // 2) as i:
                for q in range(2):
                    from_h(i, T_ZM, q)
            with pe.Fori(0, KC) as i:
                from_h(i, T_MM)
                pe.wait_ge(y_ready, 3 * AC)
                from_y(i, T_MM)

            def out_block(i, p, first=False, last=False):
                b_no = 2 * i + p
                pe.wait_ge(drained[p], T_OUT // 2 + i)
                pe.wait_ge(mb_hi_made, b_no + 2)
                pe.wait_ge(mb_lo_made, b_no + 2)
                for half in range(2):
                    for k in range(KC):
                        if first:
                            pe.wait_ge(wo_lo_made, half * KC + k + 1)
                        n = half * KC + k
                        hi = mb_hi[:, (p * KC + k) * P:(p * KC + k + 1) * P]
                        lo = mb_lo[:, (p * KC + k) * P:(p * KC + k + 1) * P]
                        dst = pm[:, p, half * HALF:(half + 1) * HALF]
                        pe.matmul(dst, hi, wo_hi[:, n * HALF:(n + 1) * HALF], start=(k == 0), stop=False)
                        pe.matmul(dst, lo, wo_hi[:, n * HALF:(n + 1) * HALF], start=False, stop=False)
                        mm = pe.matmul(dst, hi, wo_lo[:, n * HALF:(n + 1) * HALF], start=False, stop=(k == KC - 1))
                    if half == 0 and last:
                        mm.then_inc(out_half_done, 1)
                mm.then_inc(tile_done, 1)

            out_block(0, 0, first=True)
            out_block(0, 1)
            with pe.Fori(1, NB // 2 - 1) as i:
                for p in range(2):
                    out_block(i, p)
            out_block(NB // 2 - 1, 0)
            out_block(NB // 2 - 1, 1, last=True)

        @block.scalar
        def _(act):
            def split_next(p, t_half, width=D):
                act.wait_ge(raw_landed[p], 16 * t_half + 16)
                nc.scalar.activation(w_hi[:, p, 0:width], raw[:, p, 0:width], ACT.Copy).then_inc(hi_made, 1)

            def after_tile(t0, per, i, p):
                act.wait_ge(tile_done, per * i + (t0 + 1))
                split_next(p, (per // 2) * i + (t0 + 2) // 2)

            act.wait_ge(st_cleared, 1)
            nc.scalar.activation(st[:, 11, 0:1], st[:, 10, 0:1], ACT.Sqrt)

            def high_of_h(n):
                half, k = divmod(n, KC)
                bank = [sa[:, 0, :], sa[:, 1, :], sa[:, 2, :], pv[:, :]][n % 4]
                act.wait_ge(x_turned, n + 1)
                nc.scalar.activation(h_hi[:, k, half * HALF:(half + 1) * HALF], bank, ACT.Identity,
                                     scale=gpre[:, k:k + 1]).then_inc(h_hi_made, 1)

            def square_sum(b):
                act.wait_ge(x_landed[b], 16)
                nc.scalar.activation(area_a[:, b * D:(b + 1) * D], area_m[:, b * D:(b + 1) * D],
                                     ACT.Square, accum_out=st[:, 0, b:b + 1]).then_inc(ssq_act, 1)

            def roots(pair):
                cols = slice(2 * pair, 2 * pair + 2)
                act.wait_ge(var_made, pair + 1)
                nc.scalar.activation(st[:, 2, cols], st[:, 1, cols], ACT.Sqrt).then_inc(root_made, 1)

            for b in range(4):
                square_sum(b)
                if b in (1, 3):
                    roots(b // 2)
            split_next(0, 0)
            square_sum(4)
            act.wait_ge(ident_landed, 32)
            for n in range(KC):
                high_of_h(n)
                if n in (1, 2, 3):
                    square_sum(n + 4)
                if n in (1, 3):
                    roots(2 + n // 3)
            split_next(1, 0)
            for n in range(KC, 2 * KC):
                high_of_h(n)

            act.wait_ge(h_made, 2 * KC)
            for q in range(2 + AC):
                p = q % 2
                act.wait_ge(tile_done, q + 1)
                if q == 1:
                    nc.scalar.copy(vT, pm[:, 1, :]).then_inc(drained[1], 1)
                else:
                    n = q if q == 0 else q - 1
                    if n:
                        act.wait_ge(roped, n)
                    else:
                        act.wait_ge(rope_landed, 48)
                    nc.scalar.copy(q_raw, pm[:, p, :]).then_inc(drained[p], 1)
                    act.wait_ge(drained[p], q // 2 + 1)
                    for row in (0, HEAD):
                        half_rot = ROT // 2
                        act.dma_start(q_swap[row:row + half_rot, :],
                                      q_raw[row + half_rot:row + ROT, :]).then_inc(swapped, 16)
                        act.dma_start(q_swap[row + half_rot:row + ROT, :],
                                      q_raw[row:row + half_rot, :]).then_inc(swapped, 16)
                split_next(p, (q + 2) // 2)
                if q == 2:
                    for n in range(2):
                        act.wait_ge(v_turned, n + 1)
                        nc.scalar.copy(vtok[:, 4 * n:4 * n + 4, :],
                                       sa[:, n, :].rearrange("p (b d) -> p b d", b=4)).then_inc(v_made, 1)

            def conv_tiles(j):
                act.wait_ge(tile_done, 4 * j + (T_CONV + 1))
                act.wait_ge(drained[1], 2 * j + T_CONV // 2)
                nc.scalar.copy(conv_c, pm[:, 0, :]).then_inc(drained[0], 1)
                split_next(0, 2 * j + (T_CONV + 2) // 2)
                after_tile(T_CONV + 1, 4, j, 1)
                after_tile(T_CONV + 2, 4, j, 0)

            def conv_z(j, width=D):
                act.wait_ge(tile_done, 4 * j + (T_CONV + 4))
                act.wait_ge(drained[1], 2 * j + (T_CONV // 2 + 1))
                nc.scalar.activation(sig, pm[:, 1, :], ACT.Sigmoid).then_inc(sig_made, 1)
                split_next(1, 2 * j + (T_CONV + 5) // 2, width)
                act.wait_ge(y_made, j + 1)
                nc.scalar.activation(y_hi[:, j, :], sig, ACT.Copy).then_inc(y_hi_made, 1)

            with act.Fori(0, AC - 1) as j:
                conv_tiles(j)
                conv_z(j)

            def exps(i, g):
                act.wait_ge(nm_ready, 2 * i + (g + 1))
                nc.scalar.activation(st[:, 4, 4:8], st[:, 4, 0:4], ACT.Exp)
                for h in range(GROUP):
                    ins = nc.scalar.activation(probs[:, h, :], probs[:, h, :], ACT.Exp,
                                               bias=st[:, 3, h:h + 1], accum_out=st[:, 5, h:h + 1])
                ins.then_inc(exped, 1)

            def take_probs(i, g):
                await_count(act, pv_done, 2 * i + g)
                for j, bank in enumerate(BANKS):
                    act.wait_ge(turned, 6 * i + (3 * g + j + 1))
                    nc.scalar.activation(probsT_hi[:, j, :], sa[:, bank, :], ACT.Copy).then_inc(pt_hi_made, 1)

            def merge_a(i, more=True):
                take_probs(i, 0)
                exps(i, 1)
                act.wait_ge(tile_done, 2 * i + (T_MA + 1))
                act.wait_ge(drained[1], i + T_MA // 2)
                nc.scalar.activation(sig, pm[:, 0, :], ACT.Sigmoid).then_inc(drained[0], 1)
                split_next(0, i + (T_MA + 2) // 2)
                take_probs(i, 1)
                act.wait_ge(tile_done, 2 * i + (T_MA + 2))
                split_next(1, i + (T_MA + 2) // 2, AW if more else D)

            conv_tiles(AC - 1)
            exps(0, 0)
            conv_z(AC - 1, AW)
            act.wait_ge(y_ready, AC)
            merge_a(0)
            with act.Fori(1, NB - 1) as i:
                exps(i, 0)
                merge_a(i)
            exps(NB - 1, 0)
            merge_a(NB - 1, more=False)

            def gated(i, q, t0, n0):
                p = q
                act.wait_ge(tile_done, 2 * i + (t0 + q + 1))
                act.wait_ge(y_ready, 2 * i + (n0 + q))
                nc.scalar.activation(sig, pm[:, p, :], ACT.Sigmoid).then_inc(sig_made, 1)
                split_next(p, i + (t0 + q + 2) // 2)
                act.wait_ge(y_made, 2 * i + (n0 + q + 1))
                nc.scalar.activation(y_hi[:, 2 * i + q, :], sig, ACT.Copy).then_inc(y_hi_made, 1)

            act.wait_ge(drained[1], T_ZB // 2)
            with act.Fori(0, AC // 2) as i:
                for q in range(2):
                    gated(i, q, T_ZB, AC)
            act.wait_ge(var_made, 5)
            nc.scalar.activation(st[:, 2, 0:2], st[:, 1, 0:2], ACT.Sqrt).then_inc(root_made, 1)
            for q in range(AC):
                after_tile(T_MQ + q, 2, 0, q % 2)
            for n in range(2 * MHEADS):
                p, t = n % 2, T_MEM + n
                act.wait_ge(tile_done, t + 1)
                if n < MHEADS:
                    nc.scalar.activation(mk_hi[:, n, :], pm[:, p, 0:MEM], ACT.Copy).then_inc(mk_hi_made, 1)
                elif n == 2 * MHEADS - 1:
                    nc.scalar.copy(mv, pm[:, 1, :].rearrange("p (b d) -> p b d", b=2)).then_inc(drained[1], 1)
                split_next(p, (t + 2) // 2)

            act.wait_ge(y_ready, 2 * AC)
            with act.Fori(0, KC) as i:
                act.wait_ge(mnm_ready, i + 1)
                for h in range(MHEADS):
                    ins = nc.scalar.activation(mprobs[:, h, :], sa[:, h // 2, (h % 2) * MEM:(h % 2 + 1) * MEM],
                                               ACT.Exp, bias=st[:, 3, h:h + 1], scale=float(P) ** -0.5,
                                               accum_out=st[:, 5, h:h + 1])
                ins.then_inc(mexped, 1)
                act.wait_ge(tile_done, 2 * i + (T_MB + 1))
                nc.scalar.activation(sig, pm[:, 0, :], ACT.Sigmoid).then_inc(drained[0], 1)
                split_next(0, i + (T_MB + 2) // 2)
                act.wait_ge(mturned, 2 * i + 1)
                act.wait_ge(pv_done, i + 2 * NB)
                nc.scalar.copy(mprobsT[:, 0, :, :],
                               sa[:, 0, :].rearrange("p (h q) -> p h q", h=MHEADS)).then_inc(pt_hi_made, 1)
                act.wait_ge(tile_done, 2 * i + (T_MB + 2))
                split_next(1, i + (T_MB + 2) // 2)

            act.wait_ge(merged_done, KC)
            with act.Fori(0, AC // 2) as i:
                for q in range(2):
                    gated(i, q, T_ZM, 2 * AC)

            def gate_m(i, more):
                act.wait_ge(tile_done, 2 * i + (T_MM + 1))
                act.wait_ge(merged_done, i + KC)
                nc.scalar.activation(sig, pm[:, 0, :], ACT.Sigmoid).then_inc(drained[0], 1)
                if more:
                    split_next(0, i + (T_MM + 2) // 2)
                    act.wait_ge(tile_done, 2 * i + (T_MM + 2))
                    split_next(1, i + (T_MM + 2) // 2)

            act.wait_ge(y_ready, 3 * AC)
            with act.Fori(0, KC - 1) as i:
                gate_m(i, True)
            gate_m(KC - 1, False)

            def wout_high(steps):
                for n in steps:
                    act.wait_ge(wout_landed[n // KC], 16)
                    nc.scalar.activation(wo_hi[:, n * HALF:(n + 1) * HALF], wout_raw[:, n * HALF:(n + 1) * HALF],
                                         ACT.Copy).then_inc(wo_hi_made, 1)

            def merged_high(p, at, k0=0, k1=KC):
                dst = mb_hi[:, (p * KC + k0) * P:(p * KC + k1) * P].rearrange("p (k q) -> p k q", k=k1 - k0)
                nc.scalar.activation(dst, merged[:, k0:k1, at], ACT.Copy).then_inc(mb_hi_made, 1)

            merged_high(0, slice(0, P), 0, KC - 1)
            wout_high(range(2))
            act.wait_ge(merged_done, 2 * KC)
            merged_high(0, slice(0, P), KC - 1)
            wout_high(range(2, 2 * KC))
            act.wait_ge(tile_done, T_OUT)
            merged_high(1, slice(P, 2 * P))

            def out_block(i, p, more, last=False):
                if last:
                    act.wait_ge(out_half_done, 1)
                    nc.scalar.activation(squares[:, p, 0:HALF], pm[:, p, 0:HALF], ACT.Square,
                                         accum_out=st[:, 6, 2:3]).then_inc(sq_made, 1)
                    act.wait_ge(tile_done, T_OUT + NB)
                    nc.scalar.activation(squares[:, p, HALF:D], pm[:, p, HALF:D], ACT.Square,
                                         accum_out=st[:, 6, 3:4]).then_inc(sq_made, 1)
                else:
                    act.wait_ge(tile_done, 2 * i + (T_OUT + p + 1))
                    nc.scalar.activation(squares[:, p, :], pm[:, p, :], ACT.Square,
                                         accum_out=st[:, 6, p:p + 1]).then_inc(sq_made, 1)
                if more:
                    merged_high(p, bass.ds((2 * i + (p + 2)) * P, P))
                act.wait_ge(out_var, 2 * i + (p + 1))
                nc.scalar.activation(st[:, 8, p:p + 1], st[:, 7, p:p + 1], ACT.Sqrt).then_inc(out_root, 1)

            for p in range(2):
                out_block(0, p, True)
            with act.Fori(1, NB // 2 - 1) as i:
                for p in range(2):
                    out_block(i, p, True)
            out_block(NB // 2 - 1, 0, False)
            out_block(NB // 2 - 1, 1, False, last=True)

        @block.vector
        def _(dve):
            chain = Chain(dve, dve_chain)
            link = chain.link

            def inv_root(var, root, r, t):
                link(nc.vector.reciprocal(r, root))
                link(nc.vector.tensor_tensor(t, r, r, ALU.mult))
                link(nc.vector.tensor_tensor(t, t, var, ALU.mult))
                link(nc.vector.tensor_scalar(t, t, -0.5, 1.5, ALU.mult, ALU.add))
                link(nc.vector.tensor_tensor(r, r, t, ALU.mult))

            nc.vector.memset(st[:, :, :], 0.0).then_inc(st_cleared, 1)
            dve.wait_ge(st_cleared, 1)

            def scale_pair(pair):
                cols = slice(2 * pair, 2 * pair + 2)
                dve.wait_ge(ssq_act, 2 * pair + 2)
                nc.vector.tensor_scalar(st[:, 1, cols], st[:, 0, cols], 1.0 / D, EPS, ALU.mult,
                                        ALU.add).then_inc(var_made, 1)
                dve.wait_ge(var_made, pair + 1)
                dve.wait_ge(root_made, pair + 1)
                inv_root(st[:, 1, cols], st[:, 2, cols], st[:, 9, cols], st[:, 10, cols])
                for b in range(2 * pair, 2 * pair + 2):
                    ins = nc.vector.tensor_scalar(area_m[:, b * D:(b + 1) * D], area_m[:, b * D:(b + 1) * D],
                                                  st[:, 9, b:b + 1], None, ALU.mult)
                ins.then_inc(xs_made, 1)

            scale_pair(0)
            scale_pair(1)
            dve.wait_ge(ident_landed, 32)
            for n in range(2 * KC):
                half, k = divmod(n, KC)
                cols = slice(half * HALF, (half + 1) * HALF)
                bank = [sa[:, 0, :], sa[:, 1, :], sa[:, 2, :], pv[:, :]][n % 4]
                if n in (2, 4):
                    scale_pair(n // 2 + 1)
                dve.wait_ge(h_hi_made, n + 1)
                nc.vector.scalar_tensor_tensor(out=h_lo[:, k, cols], in0=bank, scalar=gpre[:, k:k + 1],
                                               in1=h_hi[:, k, cols].bitcast(F32), op0=ALU.mult,
                                               op1=ALU.subtract).then_inc(h_made, 1)

            dve.wait_ge(rope_landed, 48)
            for n in range(1 + AC):
                dst = kT if n == 0 else qT[:, n - 1, :]
                dve.wait_ge(drained[0 if n == 0 else (n + 1) % 2], 1 if n == 0 else (n + 1) // 2 + 1)
                link(nc.vector.tensor_tensor(dst, q_raw, cosb, ALU.mult))
                dve.wait_ge(swapped, 64 * (n + 1))
                link(nc.vector.tensor_tensor(rot_t, q_swap, sinb, ALU.mult))
                nc.vector.tensor_tensor(dst, dst, rot_t, ALU.add).then_inc(roped, 1)
            dve.wait_ge(roped, 1 + AC)

            dve.wait_ge(small_landed, 64)
            nc.vector.memset(conv_cu[:, 0:1], 0.0)
            link(nc.vector.memset(conv_cu[:, SEQ + 1:SEQ + 2], 0.0))

            def tap_weight(j, tap):
                return wconv[:, tap, j:j + 1] if isinstance(j, int) else wconv[:, tap, bass.ds(j, 1)]

            def conv_tiles(j):
                dve.wait_ge(tile_done, 4 * j + (T_CONV + 2))
                dve.wait_ge(drained[0], 2 * j + (T_CONV // 2 + 1))
                nc.vector.tensor_tensor(conv_cu[:, 1:SEQ + 1], pm[:, 1, :], conv_c, ALU.mult).then_inc(drained[1], 1)
                dve.wait_ge(drained[1], 2 * j + (T_CONV // 2 + 1))
                link(nc.vector.tensor_scalar(conv_t, conv_cu[:, 0:SEQ], tap_weight(j, 0), None, ALU.mult))
                for tap in (1, 2):
                    link(nc.vector.scalar_tensor_tensor(out=conv_t, in0=conv_cu[:, tap:tap + SEQ],
                                                        scalar=tap_weight(j, tap), in1=conv_t,
                                                        op0=ALU.mult, op1=ALU.add))
                dve.wait_ge(tile_done, 4 * j + (T_CONV + 3))
                nc.vector.tensor_tensor(conv_t, pm[:, 0, :], conv_t, ALU.mult).then_inc(drained[0], 1)

            def conv_z(j):
                dve.wait_ge(sig_made, j + 1)
                dve.wait_ge(drained[0], 2 * j + (T_CONV // 2 + 2))
                nc.vector.tensor_tensor(sig, pm[:, 1, :], sig, ALU.mult).then_inc(drained[1], 1)
                dve.wait_ge(drained[1], 2 * j + (T_CONV // 2 + 2))
                nc.vector.tensor_tensor(sig, conv_t, sig, ALU.mult).then_inc(y_made, 1)
                dve.wait_ge(y_hi_made, j + 1)
                nc.vector.tensor_tensor(y_lo[:, j, :], sig, y_hi[:, j, :].bitcast(F32),
                                        ALU.subtract).then_inc(y_ready, 1)
                dve.wait_ge(y_ready, j + 1)

            with chain.loop(0, AC - 1, 3) as j:
                conv_tiles(j)
                conv_z(j)

            for part in (vwin_hi, vwin_lo):
                nc.vector.memset(part[:, :, 0, HEAD:P].bitcast(F32), 0.0)
                ins = nc.vector.memset(part[:, :, 1, 0:HEAD].bitcast(F32), 0.0)
            link(ins)

            def stage_qk(i, at, window):
                await_count(dve, qk_moved, 64 * i)
                own = [slice(g * HEAD, (g + 1) * HEAD) for g in range(2)]
                for g in range(2):
                    nc.vector.tensor_copy(q_stack[own[g], g, :, :], qT[own[g], :, at])
                    ins = nc.vector.tensor_copy(k_hi[own[g], g, :], kT[own[g], window])
                link(ins)
                for g in range(2):
                    nc.vector.tensor_tensor(q_low[own[g], :, :], qT[own[g], :, at],
                                            q_stack_f32[own[g], g, :, :], ALU.subtract)
                    ins = nc.vector.tensor_tensor(k_lo[own[g], :], kT[own[g], window],
                                                  k_hi[own[g], g, :].bitcast(F32), ALU.subtract)
                ins.then_inc(qk_staged, 1)

            def softmax_head(i, g, mask_at):
                for h in range(GROUP):
                    dve.wait_ge(scored, 8 * i + (4 * g + h + 1))
                    nc.vector.memset(st[:, 11, GROUP * g + h:GROUP * g + h + 1], 0.0)
                    nc.vector.tensor_tensor_reduce(
                        out=probs[:, h, :], in0=sa[:, BANKS[h % 3], 0:WIN], in1=maskb[:, mask_at:mask_at + WIN],
                        scale=float(HEAD) ** -0.5, scalar=-3.0e38, op0=ALU.add, op1=ALU.max,
                        accum_out=st[:, 0, h:h + 1]).then_inc(masked, 1)
                dve.wait_ge(masked, 8 * i + (4 * g + 4))
                sinks = sinkb[:, GROUP * g:GROUP * g + GROUP]
                link(nc.vector.tensor_tensor(st[:, 1, 0:4], st[:, 0, 0:4], sinks, ALU.max))
                link(nc.vector.tensor_scalar(st[:, 3, 0:4], st[:, 1, 0:4], -1.0, None, ALU.mult))
                nc.vector.tensor_tensor(st[:, 4, 0:4], sinks, st[:, 3, 0:4], ALU.add).then_inc(nm_ready, 1)

            def softmax_tail(i, g):
                dve.wait_ge(exped, 2 * i + (g + 1))
                link(nc.vector.tensor_tensor(st[:, 5, 4:8], st[:, 5, 0:4], st[:, 4, 4:8], ALU.add))
                link(nc.vector.reciprocal(st[:, 6, 0:4], st[:, 5, 4:8]))
                for h in range(GROUP):
                    ins = nc.vector.tensor_scalar(probs[:, h, :], probs[:, h, :], st[:, 6, h:h + 1], None, ALU.mult)
                ins.then_inc(p_ready, 1)

            def take_probs(i, g):
                await_count(dve, pv_done, 2 * i + g)
                for j, bank in enumerate(BANKS):
                    dve.wait_ge(pt_hi_made, 6 * i + (3 * g + j + 1))
                    nc.vector.tensor_tensor(probsT_lo[:, j, :], sa[:, bank, :], probsT_hi[:, j, :].bitcast(F32),
                                            ALU.subtract).then_inc(pt_lo_made, 1)

            def take_output(i, at):
                dve.wait_ge(pv_done, 2 * i + 2)
                nc.vector.tensor_copy(qT[:, :, at], pv[:, :].rearrange("p (c q) -> p c q", c=AC)).then_inc(o_taken, 1)

            def merge_a(i, window, mask_at, before, after, after_keys=None):
                if before is not None:
                    take_output(i - 1, before)
                cols = [slice(g * HEAD, (g + 1) * HEAD) for g in range(2)]
                for g in range(2):
                    ins = nc.vector.tensor_copy(vwin_hi[:, :, g, cols[g]], vtok[:, window, cols[g]])
                link(ins)
                for g in range(2):
                    ins = nc.vector.tensor_tensor(vwin_lo[:, :, g, cols[g]], vtok[:, window, cols[g]],
                                                  vwin_hi[:, :, g, cols[g]].bitcast(F32), ALU.subtract)
                ins.then_inc(v_staged, 1)
                softmax_tail(i, 0)
                take_probs(i, 0)
                softmax_head(i, 1, mask_at)
                if after is not None:
                    stage_qk(i + 1, after, after_keys)
                softmax_tail(i, 1)
                take_probs(i, 1)

            def gate_up_a(i):
                dve.wait_ge(tile_done, 2 * i + (T_MA + 2))
                dve.wait_ge(drained[0], i + (T_MA // 2 + 1))
                at = i if isinstance(i, int) else bass.ds(i, 1)
                nc.vector.tensor_tensor(merged[:, at, :], sig, pm[:, 1, :], ALU.mult).then_inc(drained[1], 1)

            LINKS_A = 10
            dve.wait_ge(v_made, 2)
            stage_qk(0, slice(0, P), slice(0, WIN))
            conv_tiles(AC - 1)
            softmax_head(0, 0, 2 * P)
            conv_z(AC - 1)
            merge_a(0, slice(0, 3), 2 * P, None, slice(P, 2 * P), slice(0, WIN))
            with chain.loop(1, NB - 2, LINKS_A) as i:
                softmax_head(i, 0, P)
                gate_up_a(i - 1)
                merge_a(i, bass.ds(i - 1, 3), P, bass.ds((i - 1) * P, P), bass.ds((i + 1) * P, P),
                        bass.ds(i * P, WIN))
            softmax_head(NB - 2, 0, P)
            gate_up_a(NB - 3)
            merge_a(NB - 2, slice(NB - 3, NB), P, slice((NB - 3) * P, (NB - 2) * P), slice((NB - 1) * P, SEQ),
                    slice(SEQ - WIN, SEQ))
            softmax_head(NB - 1, 0, 0)
            gate_up_a(NB - 2)
            merge_a(NB - 1, slice(NB - 3, NB), 0, slice((NB - 2) * P, (NB - 1) * P), None)
            take_output(NB - 1, slice((NB - 1) * P, SEQ))
            gate_up_a(NB - 1)
            dve.wait_ge(o_taken, NB)

            def gated(i, q, t0, n0):
                p = q
                dve.wait_ge(sig_made, 2 * i + (n0 + q + 1))
                nc.vector.tensor_tensor(sig, pm[:, p, :], sig, ALU.mult).then_inc(drained[p], 1)
                dve.wait_ge(drained[p], i + ((t0 + q) // 2 + 1))
                at = bass.ds(2 * i + q, 1)
                nc.vector.tensor_tensor(sig, qT[:, at, :], sig, ALU.mult).then_inc(y_made, 1)
                dve.wait_ge(y_hi_made, 2 * i + (n0 + q + 1))
                nc.vector.tensor_tensor(y_lo[:, at, :], sig, y_hi[:, at, :].bitcast(F32),
                                        ALU.subtract).then_inc(y_ready, 1)
                dve.wait_ge(y_ready, 2 * i + (n0 + q + 1))

            with dve.Fori(0, AC // 2) as i:
                for q in range(2):
                    gated(i, q, T_ZB, AC)
            dve.wait_ge(mem_landed, 32)
            for b in range(2):
                link(nc.vector.tensor_tensor_reduce(out=area_a[:, MNH0 + b * D:MNH0 + (b + 1) * D],
                                                    in0=memx[:, b, :], in1=memx[:, b, :], scale=1.0, scalar=0.0,
                                                    op0=ALU.mult, op1=ALU.add, accum_out=st[:, 0, b:b + 1]))
            nc.vector.tensor_scalar(st[:, 1, 0:2], st[:, 0, 0:2], 1.0 / D, EPS, ALU.mult, ALU.add).then_inc(var_made, 1)
            dve.wait_ge(var_made, 5)
            dve.wait_ge(root_made, 5)
            inv_root(st[:, 1, 0:2], st[:, 2, 0:2], st[:, 9, 0:2], st[:, 10, 0:2])
            for b in range(2):
                ins = nc.vector.tensor_scalar(memx[:, b, :], memx[:, b, :], st[:, 9, b:b + 1], None, ALU.mult)
            ins.then_inc(memx_ready, 1)
            def take_mq(q):
                dve.wait_ge(tile_done, T_MQ + q + 1)
                nc.vector.tensor_copy(qT[:, q, :], pm[:, q % 2, :]).then_inc(drained[q % 2], 1)

            take_mq(0)
            take_mq(1)
            for n in range(4):
                dve.wait_ge(mem_turned, n + 1)
                bank = [sa[:, 0, :], sa[:, 1, :], sa[:, 2, :], pv[:, :]][n]
                for kk in range(2):
                    k, part = 2 * n + kk, bank[:, kk * MEM:(kk + 1) * MEM]
                    link(nc.vector.tensor_scalar(mn_hi[:, k, :], part, gmem[:, k:k + 1], None, ALU.mult))
                    ins = nc.vector.scalar_tensor_tensor(out=mn_lo[:, k, :], in0=part, scalar=gmem[:, k:k + 1],
                                                         in1=mn_hi[:, k, :].bitcast(F32), op0=ALU.mult,
                                                         op1=ALU.subtract)
                ins.then_inc(mn_made, 1)

            def memory_low(n):
                width = AW if n == T_MB + 1 - T_MEM else D
                dve.wait_ge(lo_made, T_MEM + n)
                dve.wait_ge(hi_made, T_MEM + n + 1)
                nc.vector.tensor_tensor(w_lo[:, n % 2, 0:width], raw[:, n % 2, 0:width],
                                        w_hi[:, n % 2, 0:width].bitcast(F32), ALU.subtract).then_inc(lo_made, 1)

            take_mq(2)
            memory_low(0)
            take_mq(3)
            memory_low(1)
            for n in range(2 * MHEADS - 1):
                if n < MHEADS:
                    dve.wait_ge(mk_hi_made, n + 1)
                    nc.vector.tensor_tensor(mk_lo[:, n, :], pm[:, n % 2, 0:MEM], mk_hi[:, n, :].bitcast(F32),
                                            ALU.subtract).then_inc(drained[n % 2], 1)
                memory_low(n + 2)
            for p in range(2):
                dve.wait_ge(drained[p], T_MEM // 2)
            dve.wait_ge(tile_done, T_MB)

            def stage_mq(at):
                link(nc.vector.tensor_copy(mq_hi, qT[:, :, at]))
                nc.vector.tensor_tensor(mq_lo, qT[:, :, at], mq_hi.bitcast(F32), ALU.subtract).then_inc(mq_staged, 1)

            def merge_in(i, t0, n0):
                dve.wait_ge(tile_done, 2 * i + (t0 + 2))
                dve.wait_ge(drained[0], i + (t0 // 2 + 1))
                nc.vector.tensor_tensor(sig, sig, pm[:, 1, :], ALU.mult).then_inc(drained[1], 1)
                dve.wait_ge(drained[1], i + (t0 // 2 + 1))
                at = i if isinstance(i, int) else bass.ds(i, 1)
                nc.vector.tensor_tensor(merged[:, at, :], merged[:, at, :], sig, ALU.add).then_inc(merged_done, 1)

            def merge_b(i, here, after):
                for b in range(2):
                    dve.wait_ge(mscored, 2 * i + (b + 1))
                    link(nc.vector.tensor_reduce(st[:, 0, 2 * b:2 * b + 2],
                                                 sa[:, b, :].rearrange("p (h m) -> p h m", h=2), AX.X, ALU.max))
                nc.vector.tensor_scalar(st[:, 3, 0:4], st[:, 0, 0:4], -float(P) ** -0.5, None,
                                        ALU.mult).then_inc(mnm_ready, 1)
                if after is not None:
                    stage_mq(after)
                dve.wait_ge(mexped, i + 1)
                link(nc.vector.reciprocal(st[:, 6, 0:4], st[:, 5, 0:4]))
                for h in range(MHEADS):
                    ins = nc.vector.tensor_scalar(mprobs[:, h, :], mprobs[:, h, :], st[:, 6, h:h + 1], None, ALU.mult)
                ins.then_inc(mp_ready, 1)
                dve.wait_ge(mturned, 2 * i + 2)
                dve.wait_ge(pv_done, i + 2 * NB)
                nc.vector.tensor_copy(mprobsT[:, 1, :, :],
                                      sa[:, 1, :].rearrange("p (h q) -> p h q", h=MHEADS)).then_inc(pt_lo_made, 1)
                merge_in(i, T_MB, 0)
                dve.wait_ge(pv_done, i + (2 * NB + 1))
                nc.vector.tensor_copy(qT[:, :, here], pv[:, :].rearrange("p (h q) -> p h q", h=MHEADS)).then_inc(o_taken, 1)

            LINKS_B = 4
            stage_mq(slice(0, P))
            memory_low(2 * MHEADS + 1)
            with chain.loop(0, NB - 1, LINKS_B) as i:
                merge_b(i, bass.ds(i * P, P), bass.ds((i + 1) * P, P))
            merge_b(NB - 1, slice((NB - 1) * P, SEQ), None)
            dve.wait_ge(o_taken, 2 * NB)
            dve.wait_ge(merged_done, KC)

            with dve.Fori(0, AC // 2) as i:
                for q in range(2):
                    gated(i, q, T_ZM, 2 * AC)
            with dve.Fori(0, KC - 1) as i:
                merge_in(i, T_MM, KC)

            def wout_low(steps):
                for n in steps:
                    dve.wait_ge(wo_hi_made, n + 1)
                    nc.vector.tensor_tensor(wo_lo[:, n * HALF:(n + 1) * HALF], wout_raw[:, n * HALF:(n + 1) * HALF],
                                            wo_hi[:, n * HALF:(n + 1) * HALF].bitcast(F32),
                                            ALU.subtract).then_inc(wo_lo_made, 1)

            def merged_low(p, at, nth, k0=0, k1=KC):
                cols = slice((p * KC + k0) * P, (p * KC + k1) * P)
                dve.wait_ge(mb_hi_made, nth)
                nc.vector.tensor_tensor(mb_lo[:, cols].rearrange("p (k q) -> p k q", k=k1 - k0), merged[:, k0:k1, at],
                                        mb_hi[:, cols].bitcast(F32).rearrange("p (k q) -> p k q", k=k1 - k0),
                                        ALU.subtract).then_inc(mb_lo_made, 1)

            def last_merge(half):
                cols = slice(half * HALF, (half + 1) * HALF)
                if half == 0:
                    dve.wait_ge(up_half_done, 3 * KC)
                    link(nc.vector.tensor_tensor(sig[:, cols], sig[:, cols], pm[:, 1, cols], ALU.mult))
                else:
                    dve.wait_ge(tile_done, T_OUT)
                    nc.vector.tensor_tensor(sig[:, cols], sig[:, cols], pm[:, 1, cols], ALU.mult).then_inc(drained[1], 1)
                    dve.wait_ge(drained[1], T_OUT // 2)
                nc.vector.tensor_tensor(merged[:, KC - 1, cols], merged[:, KC - 1, cols], sig[:, cols],
                                        ALU.add).then_inc(merged_done, 1)

            dve.wait_ge(drained[0], T_OUT // 2)
            merged_low(0, slice(0, P), 1, 0, KC - 1)
            last_merge(0)
            wout_low(range(1))
            merged_low(0, slice(0, P), 2, KC - 1)
            wout_low(range(1, KC))
            last_merge(1)
            wout_low(range(KC, 2 * KC))
            merged_low(1, slice(P, 2 * P), 3)

            dve.wait_ge(gpost_landed, 16)

            def out_block(i, p, more, last=False):
                halves = [slice(0, HALF), slice(HALF, D)] if last else [slice(0, D)]

                def times_g(cols):
                    return nc.vector.tensor_tensor(tout[:, p, cols], pm[:, p, cols], gpostb[:, cols], ALU.mult)

                await_count(dve, stored[p], 16 * i)
                var, root, r, t = (st[:, n, p:p + 1] for n in (7, 8, 9, 10))
                total = st[:, 6, p:p + 1]
                if last:
                    dve.wait_ge(sq_made, NB)
                    link(times_g(halves[0]))
                    dve.wait_ge(sq_made, NB + 1)
                    link(nc.vector.tensor_tensor(total, st[:, 6, 2:3], st[:, 6, 3:4], ALU.add))
                else:
                    dve.wait_ge(sq_made, 2 * i + (p + 1))
                nc.vector.tensor_scalar(var, total, 1.0 / D, EPS, ALU.mult, ALU.add).then_inc(out_var, 1)
                dve.wait_ge(out_var, 2 * i + (p + 1))
                times_g(halves[-1]).then_inc(drained[p], 1)
                if more:
                    merged_low(p, bass.ds((2 * i + (p + 2)) * P, P), 2 * i + (p + 4))
                dve.wait_ge(out_root, 2 * i + (p + 1))
                inv_root(var, root, r, t)
                dve.wait_ge(drained[p], i + (T_OUT // 2 + 1))
                dve.wait_ge(xres_landed[p], 16 * i + 16)
                for cols in halves:
                    nc.vector.scalar_tensor_tensor(out=tout[:, p, cols], in0=tout[:, p, cols], scalar=r,
                                                   in1=raw[:, p, cols], op0=ALU.mult, op1=ALU.add).then_inc(out_ready, 1)

            for p in range(2):
                out_block(0, p, True)
            with chain.loop(1, NB // 2 - 1, 10) as i:
                for p in range(2):
                    out_block(i, p, True)
            out_block(NB // 2 - 1, 0, False)
            out_block(NB // 2 - 1, 1, False, last=True)


def _units(np_, w, order):
    rows = w.shape[0]
    u = w.reshape(rows // P, P, w.shape[1] // P, P)[:, :, order, :]
    return np_.ascontiguousarray(u.transpose(2, 1, 0, 3)).reshape(len(order), P, rows)


def _tables():
    half = ROT // 2
    inv = np.power(np.float64(ROPE_THETA), -np.arange(half) * (2.0 / ROT)).astype(np.float32)
    ang = (np.arange(SEQ, dtype=np.float32)[None, :] * inv[:, None]).astype(np.float64)
    cos, sin = np.ones((P, SEQ), np.float32), np.zeros((P, SEQ), np.float32)
    for row in (0, HEAD):
        cos[row:row + half] = cos[row + half:row + ROT] = np.cos(ang)
        sin[row:row + half], sin[row + half:row + ROT] = -np.sin(ang), np.sin(ang)
    q, k = np.arange(P)[:, None], np.arange(P)[None, :]
    none = np.full((P, P), -1e30, np.float32)
    left = np.where(k >= q, 0, none).astype(np.float32)
    right = np.where(k <= q, 0, none).astype(np.float32)
    strip = np.concatenate([none, left, np.zeros((P, P), np.float32), right, none], axis=1)
    return cos, sin, strip, np.eye(P, dtype=np.float32)


def kernel(x, mem, g_pre, w_in, w_conv, attn_sink, g_mem, w_mem_kv, w_up_a, w_up_b, w_up_m, w_out, g_post):
    import concourse.bacc as bacc
    from concourse.bass_utils import run_bass_kernel_spmd as run

    w_in = np.asarray(w_in)[0]
    pair = np.concatenate([np.r_[c * HEAD:(c + 1) * HEAD, (c + GROUP) * HEAD:(c + GROUP + 1) * HEAD]
                           for c in range(AC)])
    start = np.cumsum([0, AW, AW, AW, AW, AW, P, P, AW, AW, AW])
    a_b, a_c, a_x, a_z, b_q, b_k, b_v, b_z, m_q, m_z, gates = start
    cols = [np.arange(b_k, b_k + P), np.arange(b_v, b_v + P), b_q + pair]
    for c in range(AC):
        cols += [np.arange(s + c * P, s + (c + 1) * P) for s in (a_c, a_x, a_b, a_z)]
    cols += [np.arange(gates, gates + D), b_z + pair, np.arange(m_q, m_q + AW),
             np.arange(gates + D, gates + 2 * D), np.arange(m_z, m_z + AW),
             np.arange(gates + 2 * D, gates + 3 * D)]
    w8 = _units(np, w_in[:, np.concatenate(cols)], np.arange(w_in.shape[1] // P))
    wup = np.concatenate([_units(np, w, np.arange(KC)) for w in
                          (np.asarray(w_up_a)[0], np.asarray(w_up_b)[0][pair], np.asarray(w_up_m)[0])])
    w_kv = np.asarray(w_mem_kv)[0]
    wmem = np.concatenate([_units(np, w_kv, np.arange(MHEADS)),
                           w_kv[:, AW:].reshape(MHEADS, 2, P, AW).transpose(0, 2, 1, 3).reshape(MHEADS, P, D)])
    wout = np.ascontiguousarray(np.asarray(w_out)[0].reshape(KC, P, 2, HALF).transpose(2, 1, 0, 3)
                                ).reshape(2, P, KC * HALF)
    cos, sin, strip, eye = _tables()

    def columns(g):
        return np.ascontiguousarray(np.asarray(g)[0].reshape(-1, P).T)

    arrays = {
        "x": np.asarray(x)[0], "mem": np.asarray(mem)[0], "w8": w8, "wup": wup, "wmem": wmem, "wout": wout,
        "g_pre": columns(g_pre), "g_mem": columns(g_mem),
        "g_post": np.ascontiguousarray(np.broadcast_to(np.asarray(g_post)[0], (P, D))),
        "w_conv": np.ascontiguousarray(np.asarray(w_conv)[0].reshape(3, AC, P).transpose(2, 0, 1)),
        "sink": np.ascontiguousarray(np.broadcast_to(np.asarray(attn_sink)[0], (P, HEADS))),
        "cos": cos, "sin": sin, "mask": strip, "ident": eye,
    }
    nc = bacc.Bacc("TRN2", target_bir_lowering=False, num_devices=1)
    ins = [nc.dram_tensor(f"in_{n}", a.shape, F32, kind="ExternalInput").ap() for n, a in arrays.items()]
    out = nc.dram_tensor("out_0", (SEQ, D), F32, kind="ExternalOutput").ap()
    hybrid_layer(nc, *ins, out)
    r = run(nc, [{f"in_{n}": np.ascontiguousarray(a) for n, a in arrays.items()}], core_ids=[0])
    return r.results[0]["out_0"].reshape(1, SEQ, D)
```
